# Optimizing a Trainium2 kernel written in Bass

```python
import jax, jax.numpy as jnp
from jax import lax
import numpy as np

D_MODEL = 1024
BATCH = 1
SEQ = 512
DEPTH = 2

GRID_W = 64
CTX_LEN = 256
HEAD_DIM = 64
N_HEADS = D_MODEL // HEAD_DIM
A_HEADS = 3 * N_HEADS // 8
A_KV = 2
B_HEADS = N_HEADS // 4
C_HEADS = N_HEADS - A_HEADS - B_HEADS
C_KV = 2
MIX_WIDTH = N_HEADS * HEAD_DIM
WINDOW = 128
A_BLOCK = 128
NA_KH = 8
NA_KW = 16
NA_QCOLS = 16
NA_SLAB = NA_QCOLS + NA_KW
C_BLOCK = 128
FFN_HIDDEN = ((8 * D_MODEL + 3 * 256 - 1) // (3 * 256)) * 256
ROPE_THETA = 10000.0
EPS = 1e-6
NEG_INF = -1e30
_IN_WIDTHS = (A_HEADS * HEAD_DIM, A_KV * HEAD_DIM, A_KV * HEAD_DIM,
              B_HEADS * HEAD_DIM, B_HEADS * HEAD_DIM, B_HEADS * HEAD_DIM,
              C_HEADS * HEAD_DIM, C_KV * HEAD_DIM, C_KV * HEAD_DIM)
IN_WIDTH = sum(_IN_WIDTHS)
IN_SPLIT_POINTS = tuple(int(v) for v in np.cumsum(_IN_WIDTHS)[:-1])

kernel_name = 'hymba_style_diffusion_hybrid_block'

def rms_norm(x, g):
    xf = x.astype(jnp.float32)
    y = xf * lax.rsqrt(jnp.mean(xf * xf, axis=-1, keepdims=True) + EPS)
    return (y * g.astype(jnp.float32)).astype(x.dtype)

def modulate(h, shift, scale):
    return h * (1 + scale) + shift

def axial_rope_tables(L):
    t = jnp.arange(L, dtype=jnp.int32)
    row = (t // GRID_W).astype(jnp.float32)
    col = (t % GRID_W).astype(jnp.float32)
    n_freq = HEAD_DIM // 4
    inv = ROPE_THETA ** (-jnp.arange(n_freq, dtype=jnp.float32) / n_freq)
    ang = jnp.concatenate([row[:, None] * inv[None, :], col[:, None] * inv[None, :]], axis=-1)
    return jnp.cos(ang), jnp.sin(ang)

def apply_rope(x, cos, sin):
    half = HEAD_DIM // 2
    shape = (cos.shape[0],) + (1,) * (x.ndim - 3) + (half,)
    cos = cos.reshape(shape).astype(x.dtype)
    sin = sin.reshape(shape).astype(x.dtype)
    x1, x2 = x[..., :half], x[..., half:]
    return jnp.concatenate([x1 * cos - x2 * sin, x2 * cos + x1 * sin], axis=-1)

def split_mixer_inputs(proj, qk_g):
    B, L, _ = proj.shape
    hd = HEAD_DIM
    q_w, k_w, v_w, q_n, k_n, v_n, q_g, k_g, v_g = jnp.split(proj, IN_SPLIT_POINTS, axis=-1)
    q_w = rms_norm(q_w.reshape(B, L, A_KV, A_HEADS // A_KV, hd), qk_g[0])
    k_w = rms_norm(k_w.reshape(B, L, A_KV, hd), qk_g[1])
    v_w = v_w.reshape(B, L, A_KV, hd)
    q_n = rms_norm(q_n.reshape(B, L, B_HEADS, 1, hd), qk_g[2])
    k_n = rms_norm(k_n.reshape(B, L, B_HEADS, hd), qk_g[3])
    v_n = v_n.reshape(B, L, B_HEADS, hd)
    q_g = rms_norm(q_g.reshape(B, L, C_KV, C_HEADS // C_KV, hd), qk_g[4])
    k_g = rms_norm(k_g.reshape(B, L, C_KV, hd), qk_g[5])
    v_g = v_g.reshape(B, L, C_KV, hd)
    return q_w, k_w, v_w, q_n, k_n, v_n, q_g, k_g, v_g

def context_attention(q, k, v, sink=None):
    B, Lq, Hkv, G, dh = q.shape
    s = jnp.einsum('bqhgd,bkhd->bhgqk', q, k).astype(jnp.float32) * (dh ** -0.5)
    if sink is not None:
        s_sink = jnp.broadcast_to(sink.astype(jnp.float32).reshape(1, Hkv, G, 1, 1), s.shape[:-1] + (1,))
        s = jnp.concatenate([s, s_sink], axis=-1)
    p = jax.nn.softmax(s, axis=-1)[..., :k.shape[1]].astype(v.dtype)
    o = jnp.einsum('bhgqk,bkhd->bqhgd', p, v)
    return o.reshape(B, Lq, Hkv * G * dh)

def window_attention(q, k, v, kt, vt, sink):
    B, L, Hkv, G, dh = q.shape
    nb = L // A_BLOCK
    qb = q.reshape(B, nb, A_BLOCK, Hkv, G, dh)
    pad = ((0, 0), (A_BLOCK, A_BLOCK), (0, 0), (0, 0))
    kp = jnp.pad(k, pad).reshape(B, nb + 2, A_BLOCK, Hkv, dh)
    vp = jnp.pad(v, pad).reshape(B, nb + 2, A_BLOCK, Hkv, dh)
    kb = jnp.concatenate([kp[:, :-2], kp[:, 1:-1], kp[:, 2:]], axis=2)
    vb = jnp.concatenate([vp[:, :-2], vp[:, 1:-1], vp[:, 2:]], axis=2)
    qpos = jnp.arange(L).reshape(nb, A_BLOCK)
    kpos = jnp.arange(nb)[:, None] * A_BLOCK + jnp.arange(-A_BLOCK, 2 * A_BLOCK)[None, :]
    valid = ((kpos[:, None, :] >= 0) & (kpos[:, None, :] < L)
             & (jnp.abs(qpos[:, :, None] - kpos[:, None, :]) <= WINDOW))
    scale = dh ** -0.5
    s_loc = jnp.einsum('bnqhgd,bnkhd->bnhgqk', qb, kb).astype(jnp.float32) * scale
    s_loc = jnp.where(valid[None, :, None, None], s_loc, NEG_INF)
    s_ctx = jnp.einsum('bnqhgd,bkhd->bnhgqk', qb, kt).astype(jnp.float32) * scale
    s_sink = jnp.broadcast_to(sink.astype(jnp.float32).reshape(1, 1, Hkv, G, 1, 1), s_loc.shape[:-1] + (1,))
    p = jax.nn.softmax(jnp.concatenate([s_loc, s_ctx, s_sink], axis=-1), axis=-1).astype(v.dtype)
    n_loc = 3 * A_BLOCK
    n_ctx = kt.shape[1]
    o = (jnp.einsum('bnhgqk,bnkhd->bnqhgd', p[..., :n_loc], vb)
         + jnp.einsum('bnhgqk,bkhd->bnqhgd', p[..., n_loc:n_loc + n_ctx], vt))
    return o.reshape(B, L, Hkv * G * dh)

def neighbourhood_attention(q, k, v, kt, vt, rpb):
    B, L, H, _, dh = q.shape
    rows = L // GRID_W
    kh = min(NA_KH, rows)
    ncb = GRID_W // NA_QCOLS
    r = jnp.arange(rows)
    key_rows = jnp.clip(r - kh // 2, 0, rows - kh)[:, None] + jnp.arange(kh)[None, :]
    q_cols = jnp.arange(ncb)[:, None] * NA_QCOLS + jnp.arange(NA_QCOLS)[None, :]
    key_cols = (jnp.clip(jnp.arange(ncb) * NA_QCOLS - NA_KW // 2, 0, GRID_W - NA_SLAB)[:, None]
                + jnp.arange(NA_SLAB)[None, :])
    win_start = jnp.clip(q_cols - NA_KW // 2, 0, GRID_W - NA_KW)
    col_in = ((key_cols[:, None, :] >= win_start[:, :, None])
              & (key_cols[:, None, :] < win_start[:, :, None] + NA_KW))
    n_loc = kh * NA_SLAB
    valid = jnp.broadcast_to(col_in[:, :, None, :], (ncb, NA_QCOLS, kh, NA_SLAB)).reshape(ncb, NA_QCOLS, n_loc)
    idx_r = key_rows[:, None, :, None]
    idx_c = key_cols[None, :, None, :]
    k_nb = k.reshape(B, rows, GRID_W, H, dh)[:, idx_r, idx_c].reshape(B, rows, ncb, n_loc, H, dh)
    v_nb = v.reshape(B, rows, GRID_W, H, dh)[:, idx_r, idx_c].reshape(B, rows, ncb, n_loc, H, dh)
    qg = q.reshape(B, rows, ncb, NA_QCOLS, H, dh)
    dr = key_rows - r[:, None] + (NA_KH - 1)
    dc = jnp.clip(key_cols[:, None, :] - q_cols[:, :, None] + (NA_KW - 1), 0, 2 * NA_KW - 2)
    bias = rpb[:, dr[:, None, None, :, None], dc[None, :, :, None, :]]
    bias = jnp.transpose(bias.reshape(H, rows, ncb, NA_QCOLS, n_loc), (1, 2, 0, 3, 4)).astype(jnp.float32)
    scale = dh ** -0.5
    s_loc = jnp.einsum('brcqhd,brckhd->brchqk', qg, k_nb).astype(jnp.float32) * scale + bias[None]
    s_loc = jnp.where(valid[None, None, :, None], s_loc, NEG_INF)
    s_ctx = jnp.einsum('brcqhd,bkhd->brchqk', qg, kt).astype(jnp.float32) * scale
    p = jax.nn.softmax(jnp.concatenate([s_loc, s_ctx], axis=-1), axis=-1).astype(v.dtype)
    o = (jnp.einsum('brchqk,brckhd->brcqhd', p[..., :n_loc], v_nb)
         + jnp.einsum('brchqk,bkhd->brcqhd', p[..., n_loc:], vt))
    return o.reshape(B, L, H * dh)

def global_block_attention(q, k, v, kt, vt):
    B, L, Hkv, G, dh = q.shape
    nb = L // C_BLOCK
    qb = jnp.moveaxis(q.reshape(B, nb, C_BLOCK, Hkv, G, dh), 1, 0)
    k_all = jnp.concatenate([k, kt], axis=1)
    v_all = jnp.concatenate([v, vt], axis=1)
    scale = dh ** -0.5

    def block(q_blk):
        s = jnp.einsum('bqhgd,bkhd->bhgqk', q_blk, k_all).astype(jnp.float32) * scale
        p = jax.nn.softmax(s, axis=-1).astype(v_all.dtype)
        return jnp.einsum('bhgqk,bkhd->bqhgd', p, v_all)

    o = lax.map(block, qb)
    return jnp.moveaxis(o, 0, 1).reshape(B, L, Hkv * G * dh)

def swiglu(h, w_gate, w_up, w_down):
    return (jax.nn.silu(h @ w_gate) * (h @ w_up)) @ w_down

def trunk_layer(x, xt, silu_c, silu_ct, w_mod, b_mod, g_attn, g_ffn, w_in, qk_g, sink, rpb,
                w_out, w_gate, w_up, w_down, cos, sin, update_ctx):
    sh_a, sc_a, ga_a, sh_f, sc_f, ga_f = jnp.split((silu_c @ w_mod + b_mod)[:, None, :], 6, axis=-1)
    tsh_a, tsc_a, tga_a, tsh_f, tsc_f, tga_f = jnp.split(silu_ct @ w_mod + b_mod, 6, axis=-1)
    h = modulate(rms_norm(x, g_attn), sh_a, sc_a)
    ht = modulate(rms_norm(xt, g_attn), tsh_a, tsc_a)
    q_w, k_w, v_w, q_n, k_n, v_n, q_g, k_g, v_g = split_mixer_inputs(h @ w_in, qk_g)
    tq_w, tk_w, tv_w, tq_n, tk_n, tv_n, tq_g, tk_g, tv_g = split_mixer_inputs(ht @ w_in, qk_g)
    q_w, k_w = apply_rope(q_w, cos, sin), apply_rope(k_w, cos, sin)
    q_g, k_g = apply_rope(q_g, cos, sin), apply_rope(k_g, cos, sin)
    o = jnp.concatenate([window_attention(q_w, k_w, v_w, tk_w, tv_w, sink),
                         neighbourhood_attention(q_n, k_n, v_n, tk_n, tv_n, rpb),
                         global_block_attention(q_g, k_g, v_g, tk_g, tv_g)], axis=-1)
    x = x + ga_a * (o @ w_out)
    x = x + ga_f * swiglu(modulate(rms_norm(x, g_ffn), sh_f, sc_f), w_gate, w_up, w_down)
    if update_ctx:
        ot = jnp.concatenate([context_attention(tq_w, tk_w, tv_w, sink),
                              context_attention(tq_n, tk_n, tv_n),
                              context_attention(tq_g, tk_g, tv_g)], axis=-1)
        xt = xt + tga_a * (ot @ w_out)
        xt = xt + tga_f * swiglu(modulate(rms_norm(xt, g_ffn), tsh_f, tsc_f), w_gate, w_up, w_down)
    return x, xt

def setup_inputs(seed: int = 0) -> dict:
    key = jax.random.key(seed)
    ks = jax.random.split(key, 17)
    f32 = jnp.float32

    def nrm(k, shape, s):
        return jax.random.normal(k, shape, f32) * s

    return {
        'x': nrm(ks[0], (BATCH, SEQ, D_MODEL), 1.0),
        'c': nrm(ks[1], (BATCH, D_MODEL), 1.0),
        'ctx': nrm(ks[2], (BATCH, CTX_LEN, D_MODEL), 1.0),
        'c_ctx': nrm(ks[3], (D_MODEL,), 1.0),
        'w_mod': nrm(ks[4], (DEPTH, D_MODEL, 6 * D_MODEL), 0.5 * D_MODEL ** -0.5),
        'b_mod': nrm(ks[5], (DEPTH, 6 * D_MODEL), 0.01),
        'norm_attn': 1.0 + nrm(ks[6], (DEPTH, D_MODEL), 0.01),
        'norm_ffn': 1.0 + nrm(ks[7], (DEPTH, D_MODEL), 0.01),
        'w_in': nrm(ks[8], (DEPTH, D_MODEL, IN_WIDTH), D_MODEL ** -0.5),
        'qk_norm': 1.0 + nrm(ks[9], (DEPTH, 6, HEAD_DIM), 0.01),
        'sink': nrm(ks[10], (DEPTH, A_HEADS), 0.5),
        'rpb': nrm(ks[11], (DEPTH, B_HEADS, 2 * NA_KH - 1, 2 * NA_KW - 1), 0.1),
        'w_out': nrm(ks[12], (DEPTH, MIX_WIDTH, D_MODEL), MIX_WIDTH ** -0.5),
        'w_gate': nrm(ks[13], (DEPTH, D_MODEL, FFN_HIDDEN), D_MODEL ** -0.5),
        'w_up': nrm(ks[14], (DEPTH, D_MODEL, FFN_HIDDEN), D_MODEL ** -0.5),
        'w_down': nrm(ks[15], (DEPTH, FFN_HIDDEN, D_MODEL), FFN_HIDDEN ** -0.5),
    }

def reference(x, c, ctx, c_ctx, w_mod, b_mod, norm_attn, norm_ffn, w_in, qk_norm, sink, rpb,
              w_out, w_gate, w_up, w_down):
    L = x.shape[1]
    cos, sin = axial_rope_tables(L)
    silu_c = jax.nn.silu(c)
    silu_ct = jax.nn.silu(c_ctx)
    xt = ctx
    for i in range(DEPTH):
        x, xt = trunk_layer(x, xt, silu_c, silu_ct, w_mod[i], b_mod[i], norm_attn[i], norm_ffn[i],
                            w_in[i], qk_norm[i], sink[i], rpb[i], w_out[i], w_gate[i], w_up[i], w_down[i],
                            cos, sin, i < DEPTH - 1)
    return x


_drawn_inputs = setup_inputs


def setup_inputs(seed=0):
    import zlib

    import numpy as np

    out = dict(_drawn_inputs(seed))
    spreads = {}
    factors = {'b_mod': 4.519, 'norm_attn': 8.0, 'norm_ffn': 8.0, 'qk_norm': 8.0, 'sink': 8.0, 'rpb': 8.0}
    for name, (base, spread) in spreads.items():
        noise = np.random.default_rng([zlib.crc32(name.encode()), seed]).standard_normal(out[name].shape)
        drawn = base * np.exp(spread * noise) if base else spread * noise
        out[name] = __import__('jax').numpy.asarray(drawn.astype(out[name].dtype))
    for name, factor in factors.items():
        out[name] = (out[name] * factor).astype(out[name].dtype)
    return out
```

```python
from contextlib import ExitStack

import numpy as np

import concourse.bass as bass
from concourse import mybir

F32 = mybir.dt.float32
F32R = mybir.dt.float32r
F16 = mybir.dt.float16
BF16 = mybir.dt.bfloat16
ALU = mybir.AluOpType
ACT = mybir.ActivationFunctionType
AX_X = mybir.AxisListType.X

P = 128
D = 1024
KT = D // P
LAT, CTX = 512, 256
TOK = LAT + CTX
DEPTH = 2
GRID_W, ROWS = 64, 8
HD = 64
FT = 22
CHUNKS = [8, 8, 6]
EPS = 1e-6
SCALE = HD ** -0.5
NEG = -1e30
SHIFT = 14 * float(np.log(2.0))
N_MOD = 6 * KT
MOD_FIRST = 2 * KT
N_FFN_MOD = 2 * FT
ATTN_MOD = [(0, m) for m in range(MOD_FIRST, N_MOD)] + [(1, m) for m in range(N_FFN_MOD, N_MOD)]
UNITS_PER_LAYER = 16 + KT + sum(2 * n + KT for n in CHUNKS)

A0, B0, C0 = 0, 640, 1408
QKV = (
    [("v", 0, None, (A0 + 512, A0 + 576)), ("k", 3, 1, (A0 + 384, A0 + 448))]
    + [("q", i, 0, (A0 + 64 * i, A0 + 64 * (i + 3))) for i in range(3)]
    + [("v", 1, None, (C0 + 512, C0 + 576)), ("k", 11, 5, (C0 + 384, C0 + 448))]
    + [("q", 8 + i, 4, (C0 + 64 * i, C0 + 64 * (i + 3))) for i in range(3)]
    + [("vb", i, None, (B0 + 512 + 128 * i, B0 + 576 + 128 * i)) for i in range(2)]
    + [("kb", 6 + i, 3, (B0 + 256 + 128 * i, B0 + 320 + 128 * i)) for i in range(2)]
    + [("qb", 4 + i, 2, (B0 + 128 * i, B0 + 64 + 128 * i)) for i in range(2)]
)
N_QK = sum(w[0] != "v" for w, *_ in QKV)
N_ROPE = sum(w in "qk" for w, *_ in QKV)
SLAB = [0, 8, 24, 32]
VARIANT = [0, 1, 1, 2]
BIAS_AT = [16, 8, 0]
V_AT = [0, 768, 1536, 2816]


def attention_steps(layer):
    out = []
    for group, q0, kt, v0, o0 in (("A", 0, 3, V_AT[0], 0), ("C", 8, 11, V_AT[1], 5)):
        for i in range(3):
            for half in range(2):
                for qb in range(4):
                    lo, hi = (max(qb - 1, 0), min(qb + 2, 4)) if group == "A" else (0, 4)
                    vs = [v0 + 128 * t + 64 * half for t in [4, 5] + list(range(lo, hi))]
                    out.append(dict(group=group, q=q0 + i, k=kt, half=half, q0=128 * qb, k0=128 * lo,
                                    local=128 * (hi - lo), v=vs, qt=qb, o=(o0 + i) * 128 + 64 * half,
                                    head=i + 3 * half, qb=qb, lo=lo))
    if layer < DEPTH - 1:
        for t in range(2):
            for o in range(8):
                for half in range(2):
                    if o < 3:
                        g, q, k, v0, hd = "A", o, 3, V_AT[0] + 512, o + 3 * half
                    elif o < 5:
                        g, q, k, v0, hd = "B", 4 + o - 3, 6 + o - 3, V_AT[2 + o - 3] + 1024, 0
                    else:
                        g, q, k, v0, hd = "C", 8 + o - 5, 11, V_AT[1] + 512, 0
                    out.append(dict(group=g, q=q, k=k, half=half, q0=LAT + 128 * t, k0=0, local=0,
                                    v=[v0 + 64 * half, v0 + 128 + 64 * half], qt=4 + t,
                                    o=o * 128 + 64 * half, head=hd, qb=None, lo=0))
    for h in range(4):
        for cb in range(4):
            v0 = V_AT[2 + h // 2] + 64 * (h % 2)
            out.append(dict(group="B", q=4 + h // 2, k=6 + h // 2, half=h % 2, q0=128 * cb,
                            k0=ROWS * SLAB[cb], local=256,
                            v=[v0 + 128 * t for t in (8, 9, 2 * cb, 2 * cb + 1)], qt=cb,
                            o=(3 + h // 2) * 128 + 64 * (h % 2), head=h, qb=cb, lo=0))
    return out


STEPS = [dict(s, layer=l, first=i == 0) for l in range(DEPTH) for i, s in enumerate(attention_steps(l))]
LAYER_STEPS = [[g for g, s in enumerate(STEPS) if s["layer"] == l] for l in range(DEPTH)]
for s in STEPS:
    s["n"] = CTX + s["local"]
    s["masks"] = []
    if s["group"] == "A" and s["local"]:
        if s["qb"] > 0:
            s["masks"].append((CTX, 0))
        if s["qb"] < 3:
            s["masks"].append((CTX + 128 * (s["qb"] + 1 - s["lo"]), 1))
    s["bias"] = s["group"] == "B" and s["local"] > 0
    s["sink"] = s["group"] == "A"


def upto(g, what):
    return sum(what(s) for s in STEPS[:g])


def n_fix(s):
    return len(s["masks"]) + s["bias"]


def two_banks(s):
    return s["n"] > 512


def is_sink(s):
    return s["sink"]


def trunk(nc, x, c, ctx, c_ctx, w_mod, b_mod, norm_attn, norm_ffn, w_in, qk_norm, sink, rpb, w_out,
          w_gate, w_up, w_down, k_ident, k_pairs, k_swap, k_cos, k_sin, k_window, k_columns, out):
    bias_dram = nc.dram_tensor("bias_rows", [DEPTH * 4 * 15, 16 * 48], F32, kind="Internal").ap()
    with ExitStack() as stack:
        at = [(nc.sbuf_base + 63) // 64 * 64]

        def place(name, shape, dt, where=None):
            size = (2 if dt in (F16, BF16) else 4) * int(np.prod(shape[1:]))
            addr = at[0] if where is None else where
            if where is None:
                at[0] += (size + 63) // 64 * 64
            return nc.alloc_sbuf_tensor_at(name, shape, dt, offset=addr)

        def sem(name):
            return stack.enter_context(nc.semaphore(name))

        x_t = place("x_t", [P, KT, TOK], F32)
        raw_w = [place(f"raw_w{i}", [P, 8, P], F32) for i in range(2)]
        split_w = [place(f"split_w{i}", [P, 2, 8, P], F32R) for i in range(2)]
        ident16 = place("ident16", [P, P], F16)
        ident = place("ident", [P, P], F32)
        pair_ones = place("pair_ones", [P, P], F32)
        swap = place("swap", [P, P], F32)
        ones = place("ones", [P, P], F32)
        cos = place("cos", [P, LAT], F32)
        sin = place("sin", [P, LAT], F32)
        window = place("window", [P, 2, P], F32)
        columns = place("columns", [P, 3, 32], F32)
        eps = place("eps", [P, 1], F32)
        o_sum = place("o_sum", [P, HD], F32)
        turnstile = place("turnstile", [P, 1], F32)
        vecs = place("vecs", [P, P + N_ROWS], F32)
        silu_c = place("silu_c", [P, 2 * KT], F32)
        sinks = place("sinks", [P, DEPTH * 6], F32)
        neg_sinks = place("neg_sinks", [P, DEPTH * 6], F32)
        mod = place("mod", [P, DEPTH, N_MOD, 2], F32)
        gain = place("gain", [P, DEPTH, 2, KT, 2], F32)
        wide = place("wide", [P, 4, ROWS, 48], F32)
        sq = [place(f"sq{i}", [P, TOK], F32) for i in range(2)]
        root = place("root", [P, TOK], F32)
        inv = place("inv", [P, TOK], F32)
        a0 = at[0]
        act = place("act", [P, 2, KT, TOK], F32R)
        mod_start = [place(f"mod_start{i}", [P, 8, 4 * P], F32, a0 + i * 16384) for i in range(3)]
        prob = [place(f"prob{i}", [P, TOK], F32, a0 + i * 3072) for i in range(3)]
        prob16 = [place(f"prob16_{i}", [P, 2, TOK], F16, a0 + 9216 + i * 3072) for i in range(3)]
        prob_t = [place(f"prob_t{i}", [P, 2, TOK], F16, a0 + 18432 + i * 3072) for i in range(2)]
        bias = [place(f"bias{i}", [P, 3, 256], F32, a0 + 24576 + i * 3072) for i in range(4)]
        stat = place("stat", [P, 5, 96], F32, a0 + 36864)
        raw_mod = [place(f"raw_mod{i}", [P, 8, P], F32, a0 + 38912 + i * 4096) for i in range(2)]
        b0 = at[0]
        qk = place("qk", [P, 12, TOK], F32)
        v = place("v", [P, 64 * 192], BF16)
        c0 = at[0]
        o = place("o", [P, 6, D], F32)
        hidden = place("hidden", [P, 2, 8, TOK], F32R, b0)
        tokens = place("tokens", [P, 6, D], F32, b0)
        raw_q = [place(f"raw_q{i}", [P, TOK], F32, c0 + i * 3072) for i in range(2)]
        q_n = [place(f"q_n{i}", [P, LAT], F32, c0 + 6144 + i * 2048) for i in range(2)]
        q_cos = [place(f"q_cos{i}", [P, LAT], F32, c0 + 10240 + i * 2048) for i in range(2)]
        q_sin = place("q_sin", [P, LAT], F32, c0 + 14336)
        v_rest = place("v_rest", [P, 1280], F32, c0 + 16384)
        scaled = [place(f"scaled{i}", [P, TOK], F32, c0 + 16384 + i * 3072) for i in range(2)]
        mod_rows = place("mod_rows", [2, MOD_FIRST * P], F32, c0 + 2048)
        mod_chunk = place("mod_chunk", [P, 8, 2 * P], F32, b0 + 49152)
        mod_acc = place("mod_acc", [P, 2, 2 * P], F32, b0 + 57344)
        silu_g = [place(f"silu_g{i}", [P, TOK], F32, c0 + i * 3072) for i in range(2)]
        prod = [place(f"prod{i}", [P, TOK], F32, c0 + 6144 + i * 3072) for i in range(2)]
        zeros = place("zeros", [P, 1, 64], F32, c0)
        rows_v = place("rows_v", [P, P], F32, c0 + 256)
        rows_c = place("rows_c", [N_ROWS, P], F32, c0 + 768)
        assert at[0] <= nc.sbuf_usable_end, (at[0], nc.sbuf_usable_end)

        acc = [stack.enter_context(nc.psum_tensor(f"acc{i}", [P, 1024], F32)) for i in range(2)]
        side = stack.enter_context(nc.psum_tensor("side", [P, 1024], F32))
        side16 = side[:, :].bitcast(F16)
        small = stack.enter_context(nc.psum_tensor("small", [P, 512], F32))
        mod_ps = stack.enter_context(nc.psum_tensor("mod_ps", [P, 512], F32))

        consts_in, zero_in, rows_in, bias_rows_in = sem("consts_in"), sem("zero_in"), sem("rows_in"), sem("bias_rows_in")
        x_in, ctx_in = sem("x_in"), sem("ctx_in")
        raw_in = [sem(f"raw_in{i}") for i in range(2)]
        mod_start_in = [sem(f"mod_start_in{i}") for i in range(3)]
        mod_start_done, mod_rows_ready, mod_first = sem("mod_start_done"), sem("mod_rows_ready"), sem("mod_first")
        mod_chunk_in, mod_step, mod_sum, mod_late = sem("mod_chunk_in"), sem("mod_step"), sem("mod_sum"), sem("mod_late")
        vecs_in = sem("vecs_in")
        mod_in = [sem(f"mod_in{i}") for i in range(2)]
        wide_in = sem("wide_in")
        out_in = sem("out_in")
        filled, zeros_set, passed = sem("filled"), sem("zeros_set"), sem("passed")
        hi_w, split_ready, unit_done = sem("hi_w"), sem("split_ready"), sem("unit_done")
        vec_ps, vec_ready, silu_c_ready = sem("vec_ps"), sem("vec_ready"), sem("silu_c_ready")
        neg_ready, ident16_ready = sem("neg_ready"), sem("ident16_ready")
        mod_done, mod_ready, gain_ready = sem("mod_done"), sem("mod_ready"), sem("gain_ready")
        xt_ps, xt_act, xt_dve = sem("xt_ps"), sem("xt_act"), sem("xt_dve")
        sq_ready, ssq_part, root_ready, inv_ready = sem("sq_ready"), sem("ssq_part"), sem("root_ready"), sem("inv_ready")
        scaled_ready, h_hi, h_lo = sem("scaled_ready"), sem("h_hi"), sem("h_lo")
        qkv_copied, q_sq, q_ssq, q_root, q_inv = sem("qkv_copied"), sem("q_sq"), sem("q_ssq"), sem("q_root"), sem("q_inv")
        q_normed, q_swapped, q_cos_ready, q_sin_ready, q_ready = (
            sem("q_normed"), sem("q_swapped"), sem("q_cos_ready"), sem("q_sin_ready"), sem("q_ready"))
        v_ps, v_ready, v_part = sem("v_ps"), sem("v_ready"), sem("v_part")
        neg_raw, prob_hi, prob_lo = sem("neg_raw"), sem("prob_hi"), sem("prob_lo")
        scores, fixed, top, neg_top, exps, sink_exp = (
            sem("scores"), sem("fixed"), sem("top"), sem("neg_top"), sem("exps"), sem("sink_exp"))
        denom, r_denom, prob_ps, prob_t0, prob_t1, o_ps, o_ready = (
            sem("denom"), sem("r_denom"), sem("prob_ps"), sem("prob_t0"), sem("prob_t1"), sem("o_ps"), sem("o_ready"))
        o_summed = sem("o_summed")
        bias_x8, bias_ready = sem("bias_x8"), sem("bias_ready")
        ot_ps, ot_hi, ot_lo = sem("ot_ps"), sem("ot_hi"), sem("ot_lo")
        resid = sem("resid")
        silu_done, prod_done, hid_hi, hid_lo = sem("silu_done"), sem("prod_done"), sem("hid_hi"), sem("hid_lo")
        y_ps, y_act, y_dve = sem("y_ps"), sem("y_act"), sem("y_dve")

        block = stack.enter_context(nc.Block())

        def u_in(l):
            return l * UNITS_PER_LAYER

        def u_out(l):
            return u_in(l) + 16

        def u_gate(l, ch):
            return u_out(l) + KT + sum(2 * n + KT for n in CHUNKS[:ch])

        def u_down(l, ch):
            return u_gate(l, ch) + 2 * CHUNKS[ch]

        def width(l):
            return TOK if l < DEPTH - 1 else LAT

        def parts(w):
            return [(0, 0, LAT), (1, LAT, TOK)][:1 if w == LAT else 2]

        def qk_before(j):
            return sum(w[0] != "v" for w, *_ in QKV[:j])

        def rope_before(j):
            return sum(w in "qk" for w, *_ in QKV[:j])

        def by_col(ap):
            return ap.rearrange("p (c r) -> p r c", r=ROWS)

        @block.sync
        def _(sp):
            sp.dma_start(tokens[:, 0:4, :], x[0].rearrange("(t p) d -> p t d", p=P)).then_inc(x_in, 16)
            sp.dma_start(tokens[:, 4:6, :], ctx[0].rearrange("(t p) d -> p t d", p=P)).then_inc(ctx_in, 16)

            for i in range(MOD_FIRST // 4):
                if i >= 3:
                    sp.wait_ge(mod_start_done, i - 2)
                sp.dma_start(mod_start[i % 3][:, :, :],
                             w_mod[0, :, 512 * i:512 * i + 512].rearrange("(k p) n -> p k n", p=P)
                             ).then_inc(mod_start_in[i % 3], 16)

            for l in range(DEPTH):
                for j, (_, _, _, cols) in enumerate(QKV):
                    if j == 4:
                        if l == 0:
                            sp.wait_ge(bias_rows_in, 16)
                        else:
                            sp.wait_ge(bias_ready, 12 * l)
                        for h in range(4):
                            for r in range(ROWS):
                                src = bass.AP(bias_dram.tensor, ((l * 4 + h) * 15 + 7 - r) * 768,
                                              [[48, 16], [768, ROWS], [1, 48]])
                                sp.dma_start(wide[r::ROWS, h, :, :], src).then_inc(wide_in, 16)
                    u = u_in(l) + j
                    if u >= 2:
                        sp.wait_ge(split_ready, u - 1)
                    for half in range(2):
                        sp.dma_start(raw_w[u % 2][:, :, 64 * half:64 * half + 64],
                                     w_in[l, :, cols[half]:cols[half] + 64].rearrange("(k p) n -> p k n", p=P)
                                     ).then_inc(raw_in[u % 2], 16)

                def load_out(u, col):
                    for half in range(2):
                        rows = raw_w[u % 2][64 * half:64 * half + 64]
                        for k0, n, r0, step in ((0, 3, 192 * half, 64), (3, 2, 384 + 64 * half, 128), (5, 3, 640 + 192 * half, 64)):
                            src = bass.AP(w_out.tensor, (l * D + r0) * D + col, [[D, 64], [step * D, n], [1, P]])
                            sp.dma_start(rows[:, k0:k0 + n, :], src).then_inc(raw_in[u % 2], 16)

                for j in range(4):
                    u = u_out(l) + j
                    sp.wait_ge(split_ready, u - 1)
                    load_out(u, P * j)
                if l == 0:
                    sp.wait_ge(unit_done, u_out(0))
                    for n, (ll, m) in enumerate(ATTN_MOD):
                        if n >= 2:
                            sp.wait_ge(mod_done, n - 1)
                        sp.dma_start(raw_mod[n % 2][:, :, :],
                                     w_mod[ll, :, P * m:P * m + P].rearrange("(k p) n -> p k n", p=P)
                                     ).then_inc(mod_in[n % 2], 16)
                for j in range(4, KT):
                    u = u_out(l) + j
                    sp.wait_ge(split_ready, u - 1)
                    load_out(u, P * j)
                for ch, n in enumerate(CHUNKS):
                    f0 = sum(CHUNKS[:ch])
                    with sp.Fori(0, n) as f:
                        for side_w, w in enumerate((w_gate, w_up)):
                            sp.wait_ge(split_ready, f * 2 + (u_gate(l, ch) + side_w - 1))
                            sp.dma_start(raw_w[side_w][:, :, :],
                                         w[l].rearrange("(k p) n -> p k n", p=P)[:, :, bass.ds(f * P + f0 * P, P)]
                                         ).then_inc(raw_in[side_w], 16)
                    with sp.Fori(0, KT // 2) as d:
                        for s in range(2):
                            sp.wait_ge(split_ready, d * 2 + (u_down(l, ch) + s - 1))
                            sp.dma_start(raw_w[s][:, 0:n, :],
                                         w_down[l, f0 * P:(f0 + n) * P, :].rearrange("(k p) n -> p k n", p=P)[:, :, bass.ds(d * (2 * P) + s * P, P)]
                                         ).then_inc(raw_in[s], 16)
            for t in range(4):
                sp.wait_ge(y_act if t % 2 == 0 else y_dve, t // 2 + 1)
                sp.dma_start(out[0, P * t:P * t + P, :], tokens[:, t, :]).then_inc(out_in, 16)
            sp.wait_ge(out_in, 64)

        def raw_at(l, stage, i):
            loads = 0
            for ll in range(DEPTH):
                for st, units, each in (("in", 16, 2), ("out", KT, 6)) + tuple(
                        x for ch, n in enumerate(CHUNKS) for x in ((("gate", ch), 2 * n, 1), (("down", ch), KT, 1))):
                    if (ll, st) == (l, stage):
                        return 16 * (loads + each * (i // 2 + 1)) if isinstance(i, int) else 16 * loads
                    loads += each * units // 2

        @block.gpsimd
        def _(pool):
            pool.memset(ones[:, :], 1.0).then_inc(filled, 1)
            pool.memset(eps[:, :], EPS).then_inc(filled, 1)
            pool.memset(zeros[:, :, :], 0.0).then_inc(zeros_set, 1)

            def split(slot, n, landed, used, hi_count):
                pool.wait_ge(raw_in[slot], landed)
                if used is not None:
                    pool.wait_ge(unit_done, used)
                if not isinstance(used, int) and used is not None:
                    pool.tensor_tensor(turnstile[:, 0:1], ones[:, 0:1], ones[:, 0:1], ALU.mult).then_inc(passed, 1)
                pool.tensor_scalar(split_w[slot][:, 0, 0:n, :], raw_w[slot][:, 0:n, :], 1.0, 0.0,
                                   ALU.mult, ALU.add).then_inc(hi_w, 1)
                pool.wait_ge(hi_w, hi_count)
                pool.tensor_tensor(split_w[slot][:, 1, 0:n, :], raw_w[slot][:, 0:n, :],
                                   split_w[slot][:, 0, 0:n, :].bitcast(F32), ALU.subtract).then_inc(split_ready, 1)

            for l in range(DEPTH):
                def rope_cos(j):
                    if not 0 <= j < 16 or QKV[j][0] not in "qk":
                        return
                    i = l * N_ROPE + rope_before(j)
                    pool.wait_ge(q_normed, l * N_QK + qk_before(j) + 1)
                    if i >= 2:
                        pool.wait_ge(q_ready, i - 1)
                    if l == 0 and i == 0:
                        pool.wait_ge(consts_in, N_CONST * 16)
                    pool.tensor_tensor(q_cos[i % 2][:, :], q_n[i % 2][:, :], cos[:, :], ALU.mult).then_inc(q_cos_ready, 1)

                for j in range(16 + 4):
                    u = u_in(l) + j
                    if j < 16:
                        split(u % 2, 8, raw_at(l, "in", j), u - 1 if u >= 2 else None, u + 1)
                    if j < 18:
                        rope_cos(j - 3)
                    if j in (16, 17):
                        split(u % 2, 8, raw_at(l, "out", j - 16), u - 1, u + 1)
                def bias_tables(h):
                    if l == 0 and h == 0:
                        pool.wait_ge(consts_in, N_CONST * 16)
                    if h == 0:
                        pool.wait_ge(wide_in, 16 * 32 * (l + 1))
                        pool.wait_ge(unit_done, u_out(l))
                    pool.tensor_scalar(wide[:, h, :, :], wide[:, h, :, :], 1.0 / SCALE, 0.0,
                                       ALU.mult, ALU.add).then_inc(bias_x8, 1)
                    pool.wait_ge(bias_x8, l * 4 + h + 1)
                    for i in range(3):
                        pool.tensor_tensor(bias[h][:, i, :].rearrange("p (c r) -> p r c", r=ROWS),
                                           wide[:, h, :, BIAS_AT[i]:BIAS_AT[i] + 32],
                                           columns[:, i:i + 1, :].broadcast_to((P, ROWS, 32)), ALU.add
                                           ).then_inc(bias_ready, 1)

                for g in LAYER_STEPS[l]:
                    i, n = g - LAYER_STEPS[l][0], STEPS[g]["n"]
                    pool.wait_ge(exps, g + 1)
                    if i >= 3:
                        pool.wait_ge(prob_ps, g - 2)
                    pool.tensor_scalar(prob16[g % 3][:, 0, 0:n], prob[g % 3][:, 0:n], 1.0, 0.0,
                                       ALU.mult, ALU.add).then_inc(prob_hi, 1)
                    pool.wait_ge(prob_hi, g + 1)
                    pool.tensor_tensor(prob16[g % 3][:, 1, 0:n], prob[g % 3][:, 0:n], prob16[g % 3][:, 0, 0:n],
                                       ALU.subtract).then_inc(prob_lo, 1)
                    if i % 8 == 7 and i // 8 < 4:
                        bias_tables(i // 8)
                for j in range(2, KT):
                    u = u_out(l) + j
                    split(u % 2, 8, raw_at(l, "out", j), u - 1, u + 1)
                for ch, n in enumerate(CHUNKS):
                    with pool.Fori(0, n) as f:
                        for s in range(2):
                            u = u_gate(l, ch) + s
                            split(s, 8, f * 16 + (raw_at(l, ("gate", ch), None) + 16), f * 2 + (u - 1), f * 2 + (u + 1))
                    with pool.Fori(0, KT // 2) as d:
                        for s in range(2):
                            u = u_down(l, ch) + s
                            split(s, n, d * 16 + (raw_at(l, ("down", ch), None) + 16), d * 2 + (u - 1), d * 2 + (u + 1))

        @block.tensor
        def _(pe):
            pe.wait_ge(vecs_in, N_VECS * 16)
            pe.transpose(small[:, 0:P], rows_v[:, :], ident[:, :])
            pe.transpose(small[:, P:P + N_ROWS], rows_c[:, :], ident[0:N_ROWS, 0:N_ROWS]).then_inc(vec_ps, 1)
            pe.wait_ge(x_in, 16)
            pe.wait_ge(ctx_in, 16)
            for k in range(KT):
                if k >= 2:
                    pe.wait_ge(xt_act if k % 2 == 0 else xt_dve, k // 2)
                for t in range(6):
                    mm = pe.transpose(acc[k % 2][:, P * t:P * t + P], tokens[:, t, P * k:P * k + P], ident[:, :])
                mm.then_inc(xt_ps, 1)

            def modulation(l, m, w):
                at_col = 2 * (N_MOD * l + m)
                for k in range(KT):
                    mm = pe.matmul(mod_ps[:, at_col:at_col + 2], w[:, k, :], silu_c[:, k::KT],
                                   start=(k == 0), stop=(k == KT - 1))
                mm.then_inc(mod_done, 1)

            def first_modulations(i):
                pe.wait_ge(mod_start_in[i % 3], 16 * (i // 3 + 1))
                if i >= 2:
                    pe.wait_ge(mod_rows_ready, i - 1)
                ps = (small, mod_ps)[i % 2]
                for k in range(KT):
                    mm = pe.matmul(ps[0:2, :], silu_c[:, k::KT], mod_start[i % 3][:, k, :],
                                   start=(k == 0), stop=(k == KT - 1))
                mm.then_inc(mod_start_done, 1)

            def sum_squares(nu, w):
                for k in range(KT):
                    pe.wait_ge(sq_ready, nu * KT + k + 1)
                    if nu == 0 and k == 0:
                        pe.wait_ge(filled, 2)
                    if w == TOK:
                        pe.matmul(side[:, 512:TOK], ones[:, :], sq[k % 2][:, 512:TOK], start=(k == 0), stop=(k == KT - 1))
                    pe.matmul(side[:, 0:512], ones[:, :], sq[k % 2][:, 0:512], start=(k == 0),
                              stop=(k == KT - 1)).then_inc(ssq_part, 1)

            def dense(slot, n, moving, w, each_k=None):
                for k in range(n):
                    if each_k:
                        each_k(k)
                    for part in (0, 1, 2):
                        for a, b in ((0, 512), (512, TOK))[:1 if w == LAT else 2]:
                            mm = pe.matmul(acc[slot][:, a:b], split_w[slot][:, part == 2, k, :],
                                           moving[:, part == 1, k, a:b],
                                           start=(k == 0 and part == 0), stop=(k == n - 1 and part == 2))
                mm.then_inc(unit_done, 1)

            for l in range(DEPTH):
                if l == 0:
                    pe.wait_ge(silu_c_ready, 1)
                    pe.wait_ge(vec_ready, 1)
                    first_modulations(0)
                sum_squares(2 * l, TOK)
                if l == 0:
                    for i in range(1, MOD_FIRST // 4):
                        first_modulations(i)
                    pe.wait_ge(mod_rows_ready, MOD_FIRST // 4)
                    for m in range(MOD_FIRST):
                        mm = pe.transpose(mod_ps[:, 2 * m:2 * m + 2], mod_rows[:, P * m:P * m + P], ident[0:2, 0:2])
                    mm.then_inc(mod_first, 1)

                def after_copy(j):
                    if not 0 <= j < 16:
                        return
                    kind, t, _, _ = QKV[j]
                    slot = (u_in(l) + j) % 2
                    if j >= 1 and QKV[j - 1][0][0] != "v":
                        pe.wait_ge(q_root, l * N_QK + qk_before(j))
                    elif j >= 1:
                        pe.wait_ge(v_ready, l * 4 + sum(w[0] == "v" for w, *_ in QKV[:j]))
                    if kind[0] == "v":
                        pe.wait_ge(qkv_copied, l * 16 + j + 1)
                        src = raw_q[slot]
                        if kind == "v":
                            for i in range(6):
                                mm = pe.transpose(side[:, P * i:P * i + P], src[:, P * i:P * i + P], ident[:, :])
                        else:
                            if t == 0:
                                pe.wait_ge(q_sin_ready, (l + 1) * N_ROPE)
                            for i in range(8):
                                a = ROWS * SLAB[i // 2] + P * (i % 2)
                                pe.transpose(side[:, P * i:P * i + P], src[:, a:a + P], ident[:, :])
                            for i in range(2):
                                mm = pe.transpose(small[:, P * i:P * i + P], src[:, LAT + P * i:LAT + P * i + P], ident[:, :])
                        mm.then_inc(v_ps, 1)
                    else:
                        pe.wait_ge(q_sq, l * N_QK + qk_before(j) + 1)
                        if kind[0] == "k" or l < DEPTH - 1:
                            pe.matmul(side[:, 512:TOK], pair_ones[:, :], sq[slot][:, 512:TOK], start=True, stop=True)
                        pe.matmul(side[:, 0:512], pair_ones[:, :], sq[slot][:, 0:512], start=True,
                                  stop=True).then_inc(q_ssq, 1)

                def after_norm(j):
                    if not 0 <= j < 16 or QKV[j][0] not in "qk":
                        return
                    i = l * N_ROPE + rope_before(j)
                    pe.wait_ge(q_normed, l * N_QK + qk_before(j) + 1)
                    if i >= 1:
                        pe.wait_ge(q_sin_ready, i)
                    pe.matmul(small[:, 0:LAT], swap[:, :], q_n[i % 2][:, :], start=True, stop=True).then_inc(q_swapped, 1)

                for j in range(18):
                    if j < 16:
                        u = u_in(l) + j
                        pe.wait_ge(split_ready, u + 1)
                        if j >= 2:
                            pe.wait_ge(qkv_copied, l * 16 + j - 1)
                            if QKV[j - 2][0][0] != "v":
                                pe.wait_ge(q_sq, l * N_QK + qk_before(j - 2) + 1)
                        elif l == 0:
                            pe.wait_ge(xt_act, 4)
                            pe.wait_ge(xt_dve, 4)
                        else:
                            pe.wait_ge(resid, 32 * l)
                        dense(u % 2, 8, act, TOK if QKV[j][0][0] != "q" else width(l),
                              (lambda k: pe.wait_ge(h_lo, 2 * l * KT + k + 1)) if j == 0 else None)
                    after_norm(j - 2)
                    after_copy(j - 1)

                def score(g):
                    s = STEPS[g]
                    if s["first"]:
                        pe.wait_ge(v_part, 16 * (l + 1))
                        pe.wait_ge(q_ready, N_ROPE * (l + 1))
                        pe.wait_ge(q_normed, N_QK * (l + 1))
                        pe.wait_ge(v_ready, 4 * (l + 1))
                        if l == 0:
                            pe.wait_ge(mod_ready, 1)
                    if g - LAYER_STEPS[l][0] >= 2:
                        pe.wait_ge(exps, g - 1)
                    r = slice(64 * s["half"], 64 * s["half"] + 64)
                    q = qk[r, s["q"], s["q0"]:s["q0"] + P]
                    mm = pe.matmul(acc[g % 2][:, 0:CTX], q, qk[r, s["k"], LAT:TOK], start=True, stop=True)
                    for a in range(0, s["local"], 256):
                        b = min(a + 256, s["local"])
                        mm = pe.matmul(acc[g % 2][:, CTX + a:CTX + b], q, qk[r, s["k"], s["k0"] + a:s["k0"] + b],
                                       start=True, stop=True)
                    mm.then_inc(scores, 1)

                def turn(g):
                    s = STEPS[g]
                    pe.wait_ge(prob_lo, g + 1)
                    if g > LAYER_STEPS[l][0]:
                        pe.wait_ge(prob_t0, g)
                        pe.wait_ge(prob_t1, g)
                    for part in range(2):
                        for t in range(s["n"] // P):
                            mm = pe.transpose(side16[:, 1024 * part + P * t:1024 * part + P * t + P],
                                              prob16[g % 3][:, part, P * t:P * t + P], ident16[:, :])
                    mm.then_inc(prob_ps, 1)

                def weigh(g):
                    s = STEPS[g]
                    pe.wait_ge(prob_t0, g + 1)
                    pe.wait_ge(prob_t1, g + 1)
                    if g > LAYER_STEPS[l][0]:
                        pe.wait_ge(o_ready, g)
                    for t, vc in enumerate(s["v"]):
                        pe.matmul(small[:, 0:192], prob_t[g % 2][:, 0, P * t:P * t + P], v[:, 3 * vc:3 * vc + 192],
                                  start=(t == 0), stop=False)
                        mm = pe.matmul(small[:, 0:128], prob_t[g % 2][:, 1, P * t:P * t + P], v[:, 3 * vc:3 * vc + 128],
                                       start=False, stop=(t == len(s["v"]) - 1))
                    mm.then_inc(o_ps, 1)

                g0, g1 = LAYER_STEPS[l][0], LAYER_STEPS[l][-1] + 1
                for g in range(g0, g1 + 4):
                    if g < g1:
                        score(g)
                        n, due = divmod(3 * (g - g0), 8)
                        if l == 0 and due < 3 and n < len(ATTN_MOD):
                            pe.wait_ge(mod_in[n % 2], 16 * (n // 2 + 1))
                            modulation(*ATTN_MOD[n], raw_mod[n % 2])
                    if g0 <= g - 3 < g1:
                        turn(g - 3)
                    if g0 <= g - 4 < g1:
                        weigh(g - 4)

                n_t = width(l) // P
                pe.wait_ge(o_ready, g1)
                for m in range(KT):
                    if m >= 2:
                        pe.wait_ge(ot_lo, l * KT + m - 1)
                    for t in range(n_t):
                        mm = pe.transpose(acc[m % 2][:, P * t:P * t + P], o[:, t, P * m:P * m + P], ident[:, :])
                    mm.then_inc(ot_ps, 1)

                pe.wait_ge(ot_lo, (l + 1) * KT)
                for j in range(KT):
                    u = u_out(l) + j
                    pe.wait_ge(split_ready, u + 1)
                    if j >= 2:
                        pe.wait_ge(resid, 32 * l + j - 1)
                    dense(u % 2, 8, act, width(l))

                sum_squares(2 * l + 1, width(l))

                for ch, n in enumerate(CHUNKS):
                    f0 = sum(CHUNKS[:ch])
                    pe.wait_ge(resid, 32 * l + KT * (ch + 1))
                    if ch == 0:
                        pe.wait_ge(h_lo, (2 * l + 2) * KT)
                    def late_modulation():
                        for a in range(2):
                            for b in range(2):
                                mm = pe.matmul(small[:, 2 * a + b:2 * a + b + 1], mod_acc[:, b, P * a:P * a + P],
                                               ones[:, 0:1], start=True, stop=True)
                        mm.then_inc(mod_sum, 1)

                    def gate_up(f, before):
                        for s, drained in ((0, silu_done), (1, prod_done)):
                            pe.wait_ge(split_ready, f * 2 + (u_gate(l, ch) + s + 1))
                            if before is not None:
                                pe.wait_ge(drained, before)
                            dense(s, 8, act, width(l))
                        if l == 0 and before is not None:
                            pe.wait_ge(mod_step, before * 16)
                            late_modulation()

                    done = l * FT + f0
                    if done == 0:
                        gate_up(0, None)
                    with pe.Fori(int(done == 0), n) as f:
                        gate_up(f, f + done)
                    pe.wait_ge(silu_done, l * FT + f0 + n)
                    pe.wait_ge(hid_lo, l * FT + f0 + n)
                    with pe.Fori(0, KT // 2) as d:
                        for s in range(2):
                            pe.wait_ge(split_ready, d * 2 + (u_down(l, ch) + s + 1))
                            pe.wait_ge(resid, d * 2 + (32 * l + KT * (ch + 1) + s - 1))
                            dense(s, n, hidden, width(l))
                if l == 0:
                    pe.wait_ge(mod_step, 16 * FT)
                    late_modulation()

            for t in range(4):
                pe.wait_ge(resid, 32 * DEPTH)
                if t >= 2:
                    pe.wait_ge(y_act if t % 2 == 0 else y_dve, t // 2)
                for k in range(KT):
                    mm = pe.transpose(acc[t % 2][:, P * k:P * k + P], x_t[:, k, P * t:P * t + P], ident[:, :])
                mm.then_inc(y_ps, 1)

        @block.scalar
        def _(sc):
            sc.dma_start(ident[:, :], k_ident[:, :]).then_inc(vecs_in, 16)
            sc.dma_start(rows_c[0:KT, :], c[0].rearrange("(k p) -> k p", p=P)).then_inc(vecs_in, 16)
            sc.dma_start(rows_c[KT:2 * KT, :], c_ctx.rearrange("(k p) -> k p", p=P)).then_inc(vecs_in, 16)
            for half in range(2):
                sc.dma_start(rows_c[2 * KT:N_ROWS, 64 * half:64 * half + 64], qk_norm.rearrange("l g d -> (l g) d")
                             ).then_inc(vecs_in, 16)
            for l in range(DEPTH):
                r = 64 * l
                sc.dma_start(rows_v[r:r + 48, :], b_mod[l].rearrange("(k p) -> k p", p=P)).then_inc(vecs_in, 16)
                sc.dma_start(rows_v[r + 48:r + 56, :], norm_attn[l].rearrange("(k p) -> k p", p=P)).then_inc(vecs_in, 16)
                sc.dma_start(rows_v[r + 56:r + 64, :], norm_ffn[l].rearrange("(k p) -> k p", p=P)).then_inc(vecs_in, 16)
            for dst, src in ((pair_ones, k_pairs), (swap, k_swap), (cos, k_cos), (sin, k_sin)):
                sc.dma_start(dst[:, :], src[:, :]).then_inc(consts_in, 16)
            sc.dma_start(window[:, :, :], k_window[:, :, :]).then_inc(consts_in, 16)
            sc.dma_start(columns[:, :, :], k_columns[:, :, :]).then_inc(consts_in, 16)
            sc.dma_start(sinks[:, :], bass.AP(sink.tensor, 0, [[0, P], [1, DEPTH * 6]])).then_inc(consts_in, 16)
            sc.wait_ge(zeros_set, 1)
            n_rows = DEPTH * 4 * 15
            sc.dma_start(bias_dram.rearrange("a (b c) -> a b c", c=64), zeros[0:n_rows, :, :].broadcast_to((n_rows, 12, 64))).then_inc(zero_in, 16)
            sc.wait_ge(zero_in, 16)
            sc.dma_start(bass.AP(bias_dram.tensor, 1, [[768, n_rows], [49, 16], [1, 31]]),
                         bass.AP(rpb.tensor, 0, [[31, n_rows], [0, 16], [1, 31]])).then_inc(bias_rows_in, 16)

            sc.wait_ge(vec_ready, 1)
            sc.activation(silu_c[:, :], vecs[:, P:P + 2 * KT], ACT.Silu).then_inc(silu_c_ready, 1)
            for k in range(0, KT, 2):
                sc.wait_ge(xt_ps, k + 1)
                sc.activation(x_t[:, k, :], acc[0][:, 0:TOK], ACT.Copy).then_inc(xt_act, 1)

            def squares(nu, w, ready):
                for k in range(KT):
                    ready(k)
                    if nu or k >= 2:
                        sc.wait_ge(ssq_part if k >= 2 else q_ssq if nu % 2 == 0 else ssq_part,
                                   nu * KT + k - 1 if k >= 2 else N_QK * (nu // 2) if nu % 2 == 0 else nu * KT)
                        if nu % 2 and k < 2:
                            sc.wait_ge(q_ssq, N_QK * (nu // 2 + 1))
                    sc.activation(sq[k % 2][:, 0:w], x_t[:, k, 0:w], ACT.Square).then_inc(sq_ready, 1)
                sc.wait_ge(ssq_part, (nu + 1) * KT)
                if nu:
                    sc.wait_ge(q_inv, N_QK * ((nu + 1) // 2))
                    sc.wait_ge(inv_ready, nu)
                sc.activation(root[:, 0:w], side[:, 0:w], ACT.Sqrt, bias=eps[:, 0:1], scale=1.0 / D).then_inc(root_ready, 1)

            def shifted(nu, l, w):
                for k in range(KT):
                    sc.wait_ge(scaled_ready, nu * KT + k + 1)
                    for b, a0_, a1_ in parts(w):
                        i = sc.activation(act[:, 0, k, a0_:a1_], scaled[k % 2][:, a0_:a1_], ACT.Identity,
                                          bias=mod[:, l, 3 * KT * (nu % 2) + k, b:b + 1])
                    i.then_inc(h_hi, 1)

            for l in range(DEPTH):
                def ready(k, l=l):
                    if l == 0:
                        sc.wait_ge(xt_act if k % 2 == 0 else xt_dve, k // 2 + 1)
                        if k == 0:
                            sc.wait_ge(filled, 2)
                    else:
                        sc.wait_ge(resid, 32 * l - KT + k + 1)
                squares(2 * l, TOK, ready)
                if l == 0:
                    for i in range(MOD_FIRST // 4):
                        sc.wait_ge(mod_start_done, i + 1)
                        sc.activation(mod_rows[:, 512 * i:512 * i + 512], (small, mod_ps)[i % 2][0:2, :],
                                      ACT.Copy).then_inc(mod_rows_ready, 1)
                shifted(2 * l, l, TOK)

                def take_root(j):
                    if not 0 <= j < 16 or QKV[j][0][0] == "v":
                        return
                    i = l * N_QK + qk_before(j)
                    w = TOK if QKV[j][0][0] == "k" else width(l)
                    sc.wait_ge(q_ssq, i + 1)
                    if qk_before(j):
                        sc.wait_ge(q_inv, i)
                    else:
                        sc.wait_ge(inv_ready, 2 * l + 1)
                    sc.activation(root[:, 0:w], side[:, 0:w], ACT.Sqrt, bias=eps[:, 0:1], scale=1.0 / HD).then_inc(q_root, 1)

                for j in range(17):
                    if j < 16:
                        kind, t, _, _ = QKV[j]
                        slot = (u_in(l) + j) % 2
                        w = TOK if kind[0] != "q" else width(l)
                        sc.wait_ge(unit_done, u_in(l) + j + 1)
                        if j >= 2 and QKV[j - 2][0][0] == "v":
                            sc.wait_ge(v_ps, l * 4 + sum(w_[0] == "v" for w_, *_ in QKV[:j - 1]))
                        elif j >= 2:
                            sc.wait_ge(q_normed, l * N_QK + qk_before(j - 1))
                        if kind == "vb":
                            sc.activation(by_col(raw_q[slot][:, 0:LAT]), acc[slot][:, 0:LAT].rearrange("p (r c) -> p r c", r=ROWS), ACT.Copy)
                            sc.activation(raw_q[slot][:, LAT:TOK], acc[slot][:, LAT:TOK], ACT.Copy).then_inc(qkv_copied, 1)
                        else:
                            sc.activation(raw_q[slot][:, 0:w], acc[slot][:, 0:w], ACT.Copy).then_inc(qkv_copied, 1)
                        if kind[0] != "v":
                            if qk_before(j) >= 2:
                                sc.wait_ge(q_ssq, l * N_QK + qk_before(j) - 1 + (QKV[j - 1][0][0] == "v") * 0)
                            else:
                                sc.wait_ge(ssq_part, (2 * l + 1) * KT)
                            sc.activation(sq[slot][:, 0:w], acc[slot][:, 0:w], ACT.Square).then_inc(q_sq, 1)
                    take_root(j - 1)

                def softmax(g):
                    s = STEPS[g]
                    i, n, li = g - LAYER_STEPS[l][0], s["n"], s["layer"] * 6 + s["head"]
                    sc.wait_ge(neg_top, g + 1)
                    if i >= 3:
                        sc.wait_ge(prob_lo, g - 2)
                    sc.activation(prob[g % 3][:, 0:n], acc[g % 2][:, 0:n], ACT.Exp, bias=stat[:, 1, i:i + 1],
                                  scale=SCALE, accum_out=stat[:, 2, i:i + 1]).then_inc(exps, 1)
                    if s["sink"]:
                        sc.activation(stat[:, 3, i:i + 1], sinks[:, li:li + 1], ACT.Exp,
                                      bias=stat[:, 1, i:i + 1]).then_inc(sink_exp, 1)

                def copy_turned(g):
                    n = STEPS[g]["n"]
                    sc.wait_ge(prob_ps, g + 1)
                    if g - LAYER_STEPS[l][0] >= 2:
                        sc.wait_ge(o_ps, g - 1)
                    sc.activation(prob_t[g % 2][:, 0, 0:n], side16[:, 0:n], ACT.Copy).then_inc(prob_t0, 1)

                g0, g1 = LAYER_STEPS[l][0], LAYER_STEPS[l][-1] + 1
                for g in range(g0, g1 + 3):
                    if g0 <= g - 3:
                        copy_turned(g - 3)
                    if g < g1:
                        softmax(g)

                w = width(l)
                for m in range(KT):
                    sc.wait_ge(ot_ps, l * KT + m + 1)
                    if m in (3, 4):
                        i = sc.activation(act[:, 0, m, 0:LAT].rearrange("p (r c) -> p c r", r=ROWS),
                                          acc[m % 2][:, 0:LAT].rearrange("p (c r) -> p c r", r=ROWS), ACT.Copy)
                        if w == TOK:
                            i = sc.activation(act[:, 0, m, LAT:TOK], acc[m % 2][:, LAT:TOK], ACT.Copy)
                    else:
                        i = sc.activation(act[:, 0, m, 0:w], acc[m % 2][:, 0:w], ACT.Copy)
                    i.then_inc(ot_hi, 1)

                squares(2 * l + 1, w, lambda k: sc.wait_ge(resid, 32 * l + k + 1))
                shifted(2 * l + 1, l, w)

                for ch, n in enumerate(CHUNKS):
                    f0 = sum(CHUNKS[:ch])
                    def gated(f, before):
                        sc.wait_ge(unit_done, f * 2 + (u_gate(l, ch) + 1))
                        sc.activation(silu_g[0][:, 0:w], acc[0][:, 0:w], ACT.Silu).then_inc(silu_done, 1)
                        if l == 0:
                            if before is not None:
                                sc.wait_ge(mod_step, before * 16)
                            sc.dma_start(mod_chunk[:, :, :],
                                         w_mod[1].rearrange("(k p) n -> p k n", p=P)[:, :, bass.ds(f * (2 * P) + f0 * 2 * P, 2 * P)]
                                         ).then_inc(mod_chunk_in, 16)
                        sc.wait_ge(prod_done, f + (l * FT + f0 + 1))
                        sc.activation(hidden[:, 0, bass.ds(f, 1), 0:w].rearrange("p a t -> p (a t)"), prod[0][:, 0:w], ACT.Copy).then_inc(hid_hi, 1)

                    done = l * FT + f0
                    if done == 0:
                        gated(0, None)
                    with sc.Fori(int(done == 0), n) as f:
                        gated(f, f + f0)

            for t in range(0, 4, 2):
                sc.wait_ge(y_ps, t + 1)
                sc.activation(tokens[:, t, :], acc[0][:, :], ACT.Copy).then_inc(y_act, 1)

        @block.vector
        def _(ve):
            ve.wait_ge(vec_ps, 1)
            ve.tensor_copy(vecs[:, :], small[:, 0:P + N_ROWS]).then_inc(vec_ready, 1)
            ve.wait_ge(consts_in, N_CONST * 16)
            ve.tensor_scalar(neg_sinks[:, :], sinks[:, :], -1.0, SHIFT, ALU.mult, ALU.add).then_inc(neg_ready, 1)
            ve.tensor_copy(ident16[:, :], ident[:, :]).then_inc(ident16_ready, 1)
            for k in range(1, KT, 2):
                ve.wait_ge(xt_ps, k + 1)
                ve.tensor_copy(x_t[:, k, :], acc[1][:, 0:TOK]).then_inc(xt_dve, 1)

            def modulations(n, l, m0, m1):
                b = vecs[:, 64 * l + m0:64 * l + m1].rearrange("p (m a) -> p m a", a=1).broadcast_to((P, m1 - m0, 2))
                ps = mod_ps[:, 2 * (N_MOD * l + m0):2 * (N_MOD * l + m1)].rearrange("p (m a) -> p m a", a=2)
                ve.tensor_tensor(mod[:, l, m0:m1, :], ps, b, ALU.add).then_inc(mod_ready, 1)

            def gains(l, which):
                m0 = KT * (1 + 3 * which)
                g = vecs[:, 64 * l + 48 + KT * which:64 * l + 56 + KT * which].rearrange("p (m a) -> p m a", a=1).broadcast_to((P, KT, 2))
                ve.scalar_tensor_tensor(out=gain[:, l, which, :, :], in0=mod[:, l, m0:m0 + KT, :], scalar=1.0, in1=g,
                                        op0=ALU.add, op1=ALU.mult).then_inc(gain_ready, 1)

            ve.wait_ge(mod_first, 1)
            ve.wait_ge(vec_ready, 1)
            modulations(0, 0, 0, MOD_FIRST)
            ve.wait_ge(mod_ready, 1)
            gains(0, 0)

            def normed(nu, l, w):
                ve.wait_ge(root_ready, nu + 1)
                ve.reciprocal(inv[:, 0:w], root[:, 0:w]).then_inc(inv_ready, 1)
                ve.wait_ge(inv_ready, nu + 1)
                ve.wait_ge(gain_ready, [1, 2, 4, 4][nu])
                if nu == 0:
                    ve.wait_ge(xt_act, 4)

                def lo(k):
                    ve.wait_ge(h_hi, nu * KT + k + 1)
                    for b, a0_, a1_ in parts(w):
                        i = ve.scalar_tensor_tensor(out=act[:, 1, k, a0_:a1_], in0=scaled[k % 2][:, a0_:a1_],
                                                    scalar=mod[:, l, 3 * KT * (nu % 2) + k, b:b + 1],
                                                    in1=act[:, 0, k, a0_:a1_].bitcast(F32), op0=ALU.add, op1=ALU.subtract)
                    i.then_inc(h_lo, 1)

                for k in range(KT):
                    if k >= 2:
                        ve.wait_ge(h_lo, nu * KT + k - 1)
                    for b, a0_, a1_ in parts(w):
                        i = ve.scalar_tensor_tensor(out=scaled[k % 2][:, a0_:a1_], in0=x_t[:, k, a0_:a1_],
                                                    scalar=gain[:, l, nu % 2, k, b:b + 1], in1=inv[:, a0_:a1_],
                                                    op0=ALU.mult, op1=ALU.mult)
                    i.then_inc(scaled_ready, 1)
                    if k:
                        lo(k - 1)
                lo(KT - 1)

            def residual(slot, xk, l, gate_tile, w):
                for b, a0_, a1_ in parts(w):
                    i = ve.scalar_tensor_tensor(out=xk[:, a0_:a1_], in0=acc[slot][:, a0_:a1_], scalar=gate_tile[:, b:b + 1],
                                                in1=xk[:, a0_:a1_], op0=ALU.mult, op1=ALU.add)
                i.then_inc(resid, 1)

            for l in range(DEPTH):
                w = width(l)
                normed(2 * l, l, TOK)

                def norm_tile(j):
                    if not 0 <= j < 16:
                        return
                    kind, t, grp, _ = QKV[j]
                    slot = (u_in(l) + j) % 2
                    if kind[0] == "v":
                        i = sum(w_[0] == "v" for w_, *_ in QKV[:j])
                        ve.wait_ge(v_ps, l * 4 + i + 1)
                        nb = 12 if kind == "v" else 20
                        b0_ = V_AT[t if kind == "v" else 2 + t] // HD
                        pieces = [(0, 12, side, 0)] if kind == "v" else [(0, 16, side, 0), (16, 20, small, 0)]
                        out_ = v[:, 192 * b0_:192 * (b0_ + nb)].rearrange("p (b s d) -> p b s d", s=3, d=HD)
                        rest = v_rest[:, 0:nb * HD].rearrange("p (b d) -> p b d", d=HD)
                        done = 4 * (l * 4 + i)
                        for b_, e_, ps, at_ in pieces:
                            mm = ve.tensor_copy(out_[:, b_:e_, 0, :], ps[:, 0:(e_ - b_) * HD].rearrange("p (b d) -> p b d", d=HD))
                        mm.then_inc(v_part, 1)
                        ve.wait_ge(v_part, done + 1)
                        ve.wait_ge(h_lo, (2 * l + 1) * KT)
                        for b_, e_, ps, at_ in pieces:
                            mm = ve.tensor_tensor(rest[:, b_:e_, :], ps[:, 0:(e_ - b_) * HD].rearrange("p (b d) -> p b d", d=HD),
                                                  out_[:, b_:e_, 0, :], ALU.subtract)
                        mm.then_inc(v_ready, 1)
                        ve.wait_ge(v_ready, l * 4 + i + 1)
                        ve.tensor_copy(out_[:, :, 1, :], rest).then_inc(v_part, 1)
                        ve.wait_ge(v_part, done + 2)
                        ve.tensor_tensor(out_[:, :, 2, :], rest, out_[:, :, 1, :], ALU.subtract).then_inc(v_part, 2)
                        return
                    i = l * N_QK + qk_before(j)
                    wq = TOK if kind[0] == "k" else w
                    ve.wait_ge(q_root, i + 1)
                    if qk_before(j):
                        ve.wait_ge(q_normed, i)
                    ve.reciprocal(inv[:, 0:wq], root[:, 0:wq]).then_inc(q_inv, 1)
                    ve.wait_ge(q_inv, i + 1)
                    g = vecs[:, P + 2 * KT + l * 6 + grp:P + 2 * KT + l * 6 + grp + 1]
                    raw = raw_q[slot]
                    ve.wait_ge(qkv_copied, l * 16 + j + 1)
                    if wq == TOK:
                        ve.scalar_tensor_tensor(out=qk[:, t, LAT:TOK], in0=raw[:, LAT:TOK], scalar=g, in1=inv[:, LAT:TOK],
                                                op0=ALU.mult, op1=ALU.mult)
                    if kind in "qk":
                        r = l * N_ROPE + rope_before(j)
                        if r >= 2:
                            ve.wait_ge(q_ready, r - 1)
                        ve.scalar_tensor_tensor(out=q_n[r % 2][:, :], in0=raw[:, 0:LAT], scalar=g, in1=inv[:, 0:LAT],
                                                op0=ALU.mult, op1=ALU.mult).then_inc(q_normed, 1)
                    else:
                        rc = dict(r=ROWS)
                        ve.scalar_tensor_tensor(out=qk[:, t, 0:LAT].rearrange("p (c r) -> p c r", **rc),
                                                in0=raw[:, 0:LAT].rearrange("p (r c) -> p c r", **rc), scalar=g,
                                                in1=inv[:, 0:LAT].rearrange("p (r c) -> p c r", **rc),
                                                op0=ALU.mult, op1=ALU.mult).then_inc(q_normed, 1)

                def rotate(j):
                    if not 0 <= j < 16 or QKV[j][0] not in "qk":
                        return
                    kind, t, _, _ = QKV[j]
                    r = l * N_ROPE + rope_before(j)
                    ve.wait_ge(q_swapped, r + 1)
                    if r:
                        ve.wait_ge(q_ready, r)
                    ve.tensor_tensor(q_sin[:, :], small[:, 0:LAT], sin[:, :], ALU.mult).then_inc(q_sin_ready, 1)
                    ve.wait_ge(q_sin_ready, r + 1)
                    ve.wait_ge(q_cos_ready, r + 1)
                    ve.tensor_tensor(qk[:, t, 0:LAT], q_cos[r % 2][:, :], q_sin[:, :], ALU.add).then_inc(q_ready, 1)

                for j in range(1, 18):
                    rotate(j - 2)
                    norm_tile(j - 1)

                def top_of(g):
                    s = STEPS[g]
                    i, n, li = g - LAYER_STEPS[l][0], s["n"], s["layer"] * 6 + s["head"]
                    ve.wait_ge(scores, g + 1)
                    for col, which in s["masks"]:
                        part = acc[g % 2][:, col:col + P]
                        ve.tensor_tensor(part, part, window[:, which, :], ALU.add).then_inc(fixed, 1)
                    if s["bias"]:
                        var = VARIANT[s["qb"]]
                        ve.wait_ge(bias_ready, 12 * l + 3 * s["head"] + 3)
                        part = acc[g % 2][:, CTX:CTX + 256]
                        ve.tensor_tensor(part, part, bias[s["head"]][:, var, :], ALU.add).then_inc(fixed, 1)
                    if n_fix(s):
                        ve.wait_ge(fixed, upto(g + 1, n_fix))
                    ve.reduce_max(stat[:, 0, i:i + 1], acc[g % 2][:, 0:n], AX_X).then_inc(top, 1)
                    ve.wait_ge(top, g + 1)
                    ve.tensor_scalar(stat[:, 1, i:i + 1], stat[:, 0, i:i + 1], -SCALE, SHIFT, ALU.mult,
                                     ALU.add).then_inc(neg_raw if s["sink"] else neg_top, 1)
                    if s["sink"]:
                        ve.wait_ge(neg_raw, upto(g + 1, is_sink))
                        ve.tensor_scalar(stat[:, 1, i:i + 1], stat[:, 1, i:i + 1], neg_sinks[:, li:li + 1], None,
                                         ALU.min).then_inc(neg_top, 1)

                def copy_turned(g):
                    n = STEPS[g]["n"]
                    ve.wait_ge(prob_ps, g + 1)
                    if g - LAYER_STEPS[l][0] >= 2:
                        ve.wait_ge(o_ps, g - 1)
                    ve.tensor_copy(prob_t[g % 2][:, 1, 0:n], side16[:, 1024:1024 + n]).then_inc(prob_t1, 1)

                def denominator(g):
                    s = STEPS[g]
                    i = g - LAYER_STEPS[l][0]
                    ve.wait_ge(exps, g + 1)
                    src = stat[:, 2, i:i + 1]
                    if s["sink"]:
                        ve.wait_ge(sink_exp, upto(g + 1, is_sink))
                        ve.tensor_tensor(stat[:, 3, i:i + 1], stat[:, 2, i:i + 1], stat[:, 3, i:i + 1], ALU.add).then_inc(denom, 1)
                        ve.wait_ge(denom, upto(g + 1, is_sink))
                        src = stat[:, 3, i:i + 1]
                    ve.reciprocal(stat[:, 4, i:i + 1], src).then_inc(r_denom, 1)

                def take_output(g):
                    s = STEPS[g]
                    i = g - LAYER_STEPS[l][0]
                    ve.wait_ge(o_ps, g + 1)
                    ve.wait_ge(r_denom, g + 1)
                    ve.tensor_reduce(o_sum[:, :], small[:, 0:3 * HD].rearrange("p (s d) -> p d s", s=3), AX_X,
                                     ALU.add).then_inc(o_summed, 1)
                    ve.wait_ge(o_summed, g + 1)
                    ve.tensor_scalar(o[:, s["qt"], s["o"]:s["o"] + HD], o_sum[:, :], stat[:, 4, i:i + 1], None,
                                     ALU.mult).then_inc(o_ready, 1)

                g0, g1 = LAYER_STEPS[l][0], LAYER_STEPS[l][-1] + 1
                for g in range(g0, g1 + 4):
                    if g < g1:
                        top_of(g)
                    if g0 <= g - 3 < g1:
                        copy_turned(g - 3)
                        denominator(g - 3)
                    if g0 <= g - 4 < g1:
                        take_output(g - 4)

                if l == 0:
                    ve.wait_ge(mod_done, len(ATTN_MOD))
                    modulations(1, 0, MOD_FIRST, N_MOD)
                    modulations(2, 1, N_FFN_MOD, N_MOD)
                    ve.wait_ge(mod_ready, 3)
                    gains(0, 1)

                for m in range(KT):
                    ve.wait_ge(ot_hi, l * KT + m + 1)
                    if m in (3, 4):
                        i = ve.tensor_tensor(act[:, 1, m, 0:LAT].rearrange("p (r c) -> p c r", r=ROWS),
                                             acc[m % 2][:, 0:LAT].rearrange("p (c r) -> p c r", r=ROWS),
                                             act[:, 0, m, 0:LAT].rearrange("p (r c) -> p c r", r=ROWS).bitcast(F32), ALU.subtract)
                        if w == TOK:
                            i = ve.tensor_tensor(act[:, 1, m, LAT:TOK], acc[m % 2][:, LAT:TOK],
                                                 act[:, 0, m, LAT:TOK].bitcast(F32), ALU.subtract)
                    else:
                        i = ve.tensor_tensor(act[:, 1, m, 0:w], acc[m % 2][:, 0:w], act[:, 0, m, 0:w].bitcast(F32), ALU.subtract)
                    i.then_inc(ot_lo, 1)

                for j in range(KT):
                    ve.wait_ge(unit_done, u_out(l) + j + 1)
                    residual(j % 2, x_t[:, j, :], l, mod[:, l, 2 * KT + j, :], w)

                normed(2 * l + 1, l, w)

                for ch, n in enumerate(CHUNKS):
                    f0 = sum(CHUNKS[:ch])
                    def product(f, before):
                        if before is not None:
                            ve.wait_ge(hid_lo, before)
                        ve.wait_ge(unit_done, f * 2 + (u_gate(l, ch) + 2))
                        ve.wait_ge(silu_done, f + (l * FT + f0 + 1))
                        ve.tensor_tensor(prod[0][:, 0:w], acc[1][:, 0:w], silu_g[0][:, 0:w], ALU.mult).then_inc(prod_done, 1)
                        ve.wait_ge(hid_hi, f + (l * FT + f0 + 1))
                        ve.tensor_tensor(hidden[:, 1, bass.ds(f, 1), 0:w].rearrange("p a t -> p (a t)"), prod[0][:, 0:w],
                                         hidden[:, 0, bass.ds(f, 1), 0:w].rearrange("p a t -> p (a t)").bitcast(F32),
                                         ALU.subtract).then_inc(hid_lo, 1)

                    def add_late(f, before):
                        ve.wait_ge(mod_sum, before)
                        m = f * 2 + (2 * f0 - 2)
                        ve.tensor_tensor(mod[:, 1, bass.ds(m, 2), :], small[:, 0:4].rearrange("p (a b) -> p a b", b=2),
                                         vecs[:, bass.ds(m + 64, 2)].rearrange("p (m a) -> p m a", a=1).broadcast_to((P, 2, 2)),
                                         ALU.add).then_inc(mod_late, 1)

                    def late_modulation(f, before):
                        ve.wait_ge(mod_chunk_in, f * 16 + 16 * (f0 + 1))
                        for k in range(KT):
                            for b in range(2):
                                if before is not None or k:
                                    ve.wait_ge(mod_step, f * 16 + (16 * f0 + 2 * k + b - 1 + (k == 0) * (1 - b)))
                                kw = dict(out=mod_acc[:, b, :], in0=mod_chunk[:, k, :], scalar=silu_c[:, b * KT + k:b * KT + k + 1])
                                if k == 0:
                                    i = ve.tensor_scalar(kw["out"], kw["in0"], kw["scalar"], None, ALU.mult)
                                else:
                                    i = ve.scalar_tensor_tensor(**kw, in1=mod_acc[:, b, :], op0=ALU.mult, op1=ALU.add)
                                i.then_inc(mod_step, 1)

                    done = l * FT + f0
                    if done == 0:
                        product(0, None)
                        late_modulation(0, None)
                    with ve.Fori(int(done == 0), n) as f:
                        product(f, f + done)
                        if l == 0:
                            add_late(f, f + f0)
                            late_modulation(f, f + f0)
                    with ve.Fori(0, KT // 2) as d:
                        for s in range(2):
                            ve.wait_ge(unit_done, d * 2 + (u_down(l, ch) + s + 1))
                            residual(s, x_t[:, bass.ds(d * 2 + s, 1), :].rearrange("p a t -> p (a t)"), l,
                                     mod[:, l, bass.ds(d * 2 + (5 * KT + s), 1), :].rearrange("p a t -> p (a t)"), w)

                if l == 0:
                    ve.wait_ge(mod_sum, FT)
                    m = N_FFN_MOD - 2
                    ve.tensor_tensor(mod[:, 1, m:m + 2, :], small[:, 0:4].rearrange("p (a b) -> p a b", b=2),
                                     vecs[:, 64 + m:66 + m].rearrange("p (m a) -> p m a", a=1).broadcast_to((P, 2, 2)),
                                     ALU.add).then_inc(mod_late, 1)
                    ve.wait_ge(mod_late, FT)
                    ve.wait_ge(mod_step, 16 * FT)
                    gains(1, 0)
                    gains(1, 1)

            for t in range(1, 4, 2):
                ve.wait_ge(y_ps, t + 1)
                ve.tensor_copy(tokens[:, t, :], acc[1][:, :]).then_inc(y_dve, 1)


N_ROWS = 2 * KT + DEPTH * 6
N_VECS = 5 + 3 * DEPTH
N_CONST = 7


def shape_constants():
    f = np.float32
    p = np.arange(P)
    ident = np.eye(P, dtype=f)
    pairs = (p[:, None] // 64 == p[None, :] // 64).astype(f)
    swap = (p[:, None] == (p[None, :] ^ 32)).astype(f)
    t = np.arange(LAT)
    inv = (f(10000.0) ** (-np.arange(16, dtype=f) / f(16))).astype(f)
    ang = np.concatenate([(t // GRID_W).astype(f)[:, None] * inv, (t % GRID_W).astype(f)[:, None] * inv], 1)
    cos = np.ascontiguousarray(np.cos(ang).astype(f).T[p % 32])
    sin = np.ascontiguousarray(np.sin(ang).astype(f).T[p % 32] * np.where(p % 64 < 32, f(-1), f(1))[:, None])
    i = np.arange(P)
    window = np.stack([np.where(i[None, :] >= i[:, None], 0, NEG), np.where(i[None, :] <= i[:, None], 0, NEG)], 1).astype(f)
    columns = np.zeros((P, 3, 32), f)
    for cb in (0, 1, 3):
        col = 16 * cb + p // ROWS
        first = np.clip(col - 8, 0, GRID_W - 16)
        key = SLAB[cb] + np.arange(32)
        ok = (key[None, :] >= first[:, None]) & (key[None, :] < first[:, None] + 16)
        columns[:, VARIANT[cb]] = np.where(ok, 0, NEG)
    return {"k_ident": ident, "k_pairs": pairs, "k_swap": swap, "k_cos": cos, "k_sin": sin.astype(f),
            "k_window": window, "k_columns": columns}


_INS = ['x', 'c', 'ctx', 'c_ctx', 'w_mod', 'b_mod', 'norm_attn', 'norm_ffn', 'w_in', 'qk_norm', 'sink', 'rpb',
        'w_out', 'w_gate', 'w_up', 'w_down']


def kernel(**inputs):
    import concourse.bacc as _bacc
    from concourse.bass_utils import run_bass_kernel_spmd as _run

    nc = _bacc.Bacc("TRN2", target_bir_lowering=False, num_devices=1)
    consts = shape_constants()
    arrays, args = {}, []
    for name in _INS + list(consts):
        a = np.ascontiguousarray(inputs[name] if name in inputs else consts[name])
        arrays[f"in_{name}"] = a
        args.append(nc.dram_tensor(f"in_{name}", a.shape, mybir.dt.from_np(a.dtype), kind="ExternalInput").ap())
    args.append(nc.dram_tensor("out_0", (1, LAT, D), F32, kind="ExternalOutput").ap())
    trunk(nc, *args)
    r = _run(nc, [arrays], core_ids=[0])
    return r.results[0]["out_0"]
```

```python
from contextlib import ExitStack

import numpy as np

import concourse.bass as bass
from concourse import mybir

F32 = mybir.dt.float32
F32R = mybir.dt.float32r
F16 = mybir.dt.float16
BF16 = mybir.dt.bfloat16
ALU = mybir.AluOpType
ACT = mybir.ActivationFunctionType
AX_X = mybir.AxisListType.X

P = 128
D = 1024
KT = D // P
LAT, CTX = 512, 256
TOK = LAT + CTX
DEPTH = 2
GRID_W, ROWS = 64, 8
HD = 64
FT = 22
CHUNKS = [8, 8, 6]
EPS = 1e-6
SCALE = HD ** -0.5
NEG = -1e30
LAG = 3
SHIFT = 14 * float(np.log(2.0))
N_MOD = 6 * KT
MOD_FIRST = 2 * KT
N_FFN_MOD = 2 * FT
ATTN_MOD = [(0, m) for m in range(MOD_FIRST, N_MOD)] + [(1, m) for m in range(N_FFN_MOD, N_MOD)]
UNITS_PER_LAYER = 16 + KT + sum(2 * n + KT for n in CHUNKS)

A0, B0, C0 = 0, 640, 1408
QKV = (
    [("v", 0, None, (A0 + 512, A0 + 576)), ("k", 3, 1, (A0 + 384, A0 + 448))]
    + [("q", i, 0, (A0 + 64 * i, A0 + 64 * (i + 3))) for i in range(3)]
    + [("v", 1, None, (C0 + 512, C0 + 576)), ("k", 11, 5, (C0 + 384, C0 + 448))]
    + [("q", 8 + i, 4, (C0 + 64 * i, C0 + 64 * (i + 3))) for i in range(3)]
    + [("vb", i, None, (B0 + 512 + 128 * i, B0 + 576 + 128 * i)) for i in range(2)]
    + [("kb", 6 + i, 3, (B0 + 256 + 128 * i, B0 + 320 + 128 * i)) for i in range(2)]
    + [("qb", 4 + i, 2, (B0 + 128 * i, B0 + 64 + 128 * i)) for i in range(2)]
)
N_QK = sum(w[0] != "v" for w, *_ in QKV)
N_ROPE = sum(w in "qk" for w, *_ in QKV)
SLAB = [0, 8, 24, 32]
VARIANT = [0, 1, 1, 2]
BIAS_AT = [16, 8, 0]
V_AT = [0, 768, 1536, 2816]


def attention_steps(layer):
    out = []
    for group, q0, kt, v0, o0 in (("A", 0, 3, V_AT[0], 0), ("C", 8, 11, V_AT[1], 5)):
        for i in range(3):
            for half in range(2):
                for qb in range(4):
                    lo, hi = (max(qb - 1, 0), min(qb + 2, 4)) if group == "A" else (0, 4)
                    vs = [v0 + 128 * t + 64 * half for t in [4, 5] + list(range(lo, hi))]
                    out.append(dict(group=group, q=q0 + i, k=kt, half=half, q0=128 * qb, k0=128 * lo,
                                    local=128 * (hi - lo), v=vs, qt=qb, o=(o0 + i) * 128 + 64 * half,
                                    head=i + 3 * half, qb=qb, lo=lo))
    if layer < DEPTH - 1:
        for t in range(2):
            for o in range(8):
                for half in range(2):
                    if o < 3:
                        g, q, k, v0, hd = "A", o, 3, V_AT[0] + 512, o + 3 * half
                    elif o < 5:
                        g, q, k, v0, hd = "B", 4 + o - 3, 6 + o - 3, V_AT[2 + o - 3] + 1024, 0
                    else:
                        g, q, k, v0, hd = "C", 8 + o - 5, 11, V_AT[1] + 512, 0
                    out.append(dict(group=g, q=q, k=k, half=half, q0=LAT + 128 * t, k0=0, local=0,
                                    v=[v0 + 64 * half, v0 + 128 + 64 * half], qt=4 + t,
                                    o=o * 128 + 64 * half, head=hd, qb=None, lo=0))
    for h in range(4):
        for cb in range(4):
            v0 = V_AT[2 + h // 2] + 64 * (h % 2)
            out.append(dict(group="B", q=4 + h // 2, k=6 + h // 2, half=h % 2, q0=128 * cb,
                            k0=ROWS * SLAB[cb], local=256,
                            v=[v0 + 128 * t for t in (8, 9, 2 * cb, 2 * cb + 1)], qt=cb,
                            o=(3 + h // 2) * 128 + 64 * (h % 2), head=h, qb=cb, lo=0))
    return out


STEPS = [dict(s, layer=l, first=i == 0) for l in range(DEPTH) for i, s in enumerate(attention_steps(l))]
LAYER_STEPS = [[g for g, s in enumerate(STEPS) if s["layer"] == l] for l in range(DEPTH)]
for s in STEPS:
    s["n"] = CTX + s["local"]
    s["masks"] = []
    if s["group"] == "A" and s["local"]:
        if s["qb"] > 0:
            s["masks"].append((CTX, 0))
        if s["qb"] < 3:
            s["masks"].append((CTX + 128 * (s["qb"] + 1 - s["lo"]), 1))
    s["bias"] = s["group"] == "B" and s["local"] > 0
    s["sink"] = s["group"] == "A"


MOD_AT = [g for g in LAYER_STEPS[0] if g >= 4 and 2 * (g - 4) % 5 < 2][:len(ATTN_MOD)]
assert len(MOD_AT) == len(ATTN_MOD)


def upto(g, what):
    return sum(what(s) for s in STEPS[:g])


def n_fix(s):
    return len(s["masks"]) + s["bias"]


def two_banks(s):
    return s["n"] > 512


def is_sink(s):
    return s["sink"]


def trunk(nc, x, c, ctx, c_ctx, w_mod, b_mod, norm_attn, norm_ffn, w_in, qk_norm, sink, rpb, w_out,
          w_gate, w_up, w_down, k_ident, k_pairs, k_swap, k_cos, k_sin, k_window, k_columns, out):
    bias_dram = nc.dram_tensor("bias_rows", [DEPTH * 4 * 15, 16 * 48], F32, kind="Internal").ap()
    with ExitStack() as stack:
        at = [(nc.sbuf_base + 63) // 64 * 64]

        def place(name, shape, dt, where=None):
            size = (2 if dt in (F16, BF16) else 4) * int(np.prod(shape[1:]))
            addr = at[0] if where is None else where
            if where is None:
                at[0] += (size + 63) // 64 * 64
            return nc.alloc_sbuf_tensor_at(name, shape, dt, offset=addr)

        def sem(name):
            return stack.enter_context(nc.semaphore(name))

        x_t = place("x_t", [P, KT, TOK], F32)
        raw_w = [place(f"raw_w{i}", [P, 8, P], F32) for i in range(2)]
        split_w = [place(f"split_w{i}", [P, 2, 8, P], F32R) for i in range(2)]
        ident16 = place("ident16", [P, P], F16)
        ident = place("ident", [P, P], F32)
        pair_ones = place("pair_ones", [P, P], F32)
        swap = place("swap", [P, P], F32)
        ones = place("ones", [P, P], F32)
        cos = place("cos", [P, LAT], F32)
        sin = place("sin", [P, LAT], F32)
        window = place("window", [P, 2, P], F32)
        columns = place("columns", [P, 3, 32], F32)
        eps = place("eps", [P, 1], F32)
        o_sum = place("o_sum", [P, HD], F32)
        turnstile = place("turnstile", [P, 1], F32)
        vecs = place("vecs", [P, P + N_ROWS], F32)
        silu_c = place("silu_c", [P, 2 * KT], F32)
        sinks = place("sinks", [P, DEPTH * 6], F32)
        neg_sinks = place("neg_sinks", [P, DEPTH * 6], F32)
        mod = place("mod", [P, DEPTH, N_MOD, 2], F32)
        gain = place("gain", [P, DEPTH, 2, KT, 2], F32)
        wide = place("wide", [P, 4, ROWS, 48], F32)
        norm_at = at[0]
        sq = [place(f"sq{i}", [P, TOK], F32) for i in range(2)]
        root = place("root", [P, TOK], F32)
        inv = place("inv", [P, TOK], F32)
        a0 = at[0]
        act = place("act", [P, 2, KT, TOK], F32R)
        mod_start = [place(f"mod_start{i}", [P, 8, 4 * P], F32, a0 + i * 16384) for i in range(3)]
        prob = [place(f"prob{i}", [P, TOK], F32, a0 + i * 3072) for i in range(3)]
        prob16 = [place(f"prob16_{i}", [P, 2, TOK], F16, a0 + 9216 + i * 3072) for i in range(3)]
        prob_t = [place(f"prob_t{i}", [P, 2, TOK], F16, a0 + 18432 + i * 3072) for i in range(2)]
        bias = [place(f"bias{i}", [P, 3, 256], F32, a0 + 24576 + i * 3072) for i in range(4)]
        stat = place("stat", [P, 5, 96], F32, a0 + 36864)
        raw_mod = [place(f"raw_mod{i}", [P, 8, P], F32, addr)
                   for i, addr in enumerate((a0 + 38912, a0 + 43008, norm_at, norm_at + 6144))]
        b0 = at[0]
        qk = place("qk", [P, 12, TOK], F32)
        v = place("v", [P, 64 * 192], BF16)
        c0 = at[0]
        o = place("o", [P, 6, D], F32)
        hidden = place("hidden", [P, 2, 8, TOK], F32R, b0)
        tokens = place("tokens", [P, 6, D], F32, b0)
        raw_q = [place(f"raw_q{i}", [P, TOK], F32, c0 + i * 3072) for i in range(2)]
        q_n = [place(f"q_n{i}", [P, LAT], F32, c0 + 6144 + i * 2048) for i in range(2)]
        q_cos = [place(f"q_cos{i}", [P, LAT], F32, c0 + 10240 + i * 2048) for i in range(2)]
        q_sin = place("q_sin", [P, LAT], F32, c0 + 14336)
        v_rest = place("v_rest", [P, 1280], F32, c0 + 16384)
        scaled = [place(f"scaled{i}", [P, TOK], F32, c0 + 16384 + i * 3072) for i in range(2)]
        mod_rows = place("mod_rows", [2, MOD_FIRST * P], F32, c0 + 2048)
        mod_row = place("mod_row", [2, P], F32, norm_at + 4096)
        mod_chunk = place("mod_chunk", [P, 8, 2 * P], F32, b0 + 49152)
        mod_acc = place("mod_acc", [P, 2, 2 * P], F32, b0 + 57344)
        silu_g = [place(f"silu_g{i}", [P, TOK], F32, c0 + i * 3072) for i in range(2)]
        prod = [place(f"prod{i}", [P, TOK], F32, c0 + 6144 + i * 3072) for i in range(2)]
        zeros = place("zeros", [P, 1, 64], F32, c0)
        rows_v = place("rows_v", [P, P], F32, c0 + 256)
        rows_c = place("rows_c", [N_ROWS, P], F32, c0 + 768)
        assert at[0] <= nc.sbuf_usable_end, (at[0], nc.sbuf_usable_end)

        acc = [stack.enter_context(nc.psum_tensor(f"acc{i}", [P, 1024], F32)) for i in range(2)]
        side = stack.enter_context(nc.psum_tensor("side", [P, 1024], F32))
        side16 = side[:, :].bitcast(F16)
        small = stack.enter_context(nc.psum_tensor("small", [P, 512], F32))
        mod_ps = stack.enter_context(nc.psum_tensor("mod_ps", [P, 512], F32))

        consts_in, zero_in, rows_in, bias_rows_in = sem("consts_in"), sem("zero_in"), sem("rows_in"), sem("bias_rows_in")
        x_in, ctx_in = sem("x_in"), sem("ctx_in")
        raw_in = [sem(f"raw_in{i}") for i in range(2)]
        mod_start_in = [sem(f"mod_start_in{i}") for i in range(3)]
        ssq_done, mod_row_ready, mod_turned = sem("ssq_done"), sem("mod_row_ready"), sem("mod_turned")
        mod_start_done, mod_rows_ready, mod_first = sem("mod_start_done"), sem("mod_rows_ready"), sem("mod_first")
        mod_chunk_in, mod_step, mod_sum, mod_late = sem("mod_chunk_in"), sem("mod_step"), sem("mod_sum"), sem("mod_late")
        vecs_in = sem("vecs_in")
        mod_in = [sem(f"mod_in{i}") for i in range(4)]
        wide_in = sem("wide_in")
        out_in = sem("out_in")
        filled, zeros_set, passed = sem("filled"), sem("zeros_set"), sem("passed")
        hi_w, split_ready, unit_done = sem("hi_w"), sem("split_ready"), sem("unit_done")
        vec_ps, vec_ready, silu_c_ready = sem("vec_ps"), sem("vec_ready"), sem("silu_c_ready")
        neg_ready, ident16_ready = sem("neg_ready"), sem("ident16_ready")
        mod_done, mod_ready, gain_ready = sem("mod_done"), sem("mod_ready"), sem("gain_ready")
        xt_ps, xt_act, xt_dve = sem("xt_ps"), sem("xt_act"), sem("xt_dve")
        sq_ready, ssq_part, root_ready, inv_ready = sem("sq_ready"), sem("ssq_part"), sem("root_ready"), sem("inv_ready")
        scaled_ready, h_hi, h_lo = sem("scaled_ready"), sem("h_hi"), sem("h_lo")
        qkv_copied, q_sq, q_ssq, q_root, q_inv = sem("qkv_copied"), sem("q_sq"), sem("q_ssq"), sem("q_root"), sem("q_inv")
        q_normed, q_swapped, q_cos_ready, q_sin_ready, q_ready = (
            sem("q_normed"), sem("q_swapped"), sem("q_cos_ready"), sem("q_sin_ready"), sem("q_ready"))
        v_ps, v_ready, v_part = sem("v_ps"), sem("v_ready"), sem("v_part")
        neg_raw, prob_hi, prob_lo = sem("neg_raw"), sem("prob_hi"), sem("prob_lo")
        scores, fixed, top, neg_top, exps, sink_exp = (
            sem("scores"), sem("fixed"), sem("top"), sem("neg_top"), sem("exps"), sem("sink_exp"))
        denom, r_denom, prob_ps, prob_t0, prob_t1, o_ps, o_ready = (
            sem("denom"), sem("r_denom"), sem("prob_ps"), sem("prob_t0"), sem("prob_t1"), sem("o_ps"), sem("o_ready"))
        o_summed = sem("o_summed")
        bias_x8, bias_ready = sem("bias_x8"), sem("bias_ready")
        ot_ps, ot_hi, ot_lo = sem("ot_ps"), sem("ot_hi"), sem("ot_lo")
        resid = sem("resid")
        silu_done, prod_done, hid_hi, hid_lo = sem("silu_done"), sem("prod_done"), sem("hid_hi"), sem("hid_lo")
        y_ps, y_act, y_dve = sem("y_ps"), sem("y_act"), sem("y_dve")

        block = stack.enter_context(nc.Block())

        def u_in(l):
            return l * UNITS_PER_LAYER

        def u_out(l):
            return u_in(l) + 16

        def u_gate(l, ch):
            return u_out(l) + KT + sum(2 * n + KT for n in CHUNKS[:ch])

        def u_down(l, ch):
            return u_gate(l, ch) + 2 * CHUNKS[ch]

        def width(l):
            return TOK if l < DEPTH - 1 else LAT

        def parts(w):
            return [(0, 0, LAT), (1, LAT, TOK)][:1 if w == LAT else 2]

        def qk_before(j):
            return sum(w[0] != "v" for w, *_ in QKV[:j])

        def rope_before(j):
            return sum(w in "qk" for w, *_ in QKV[:j])

        def by_col(ap):
            return ap.rearrange("p (c r) -> p r c", r=ROWS)

        @block.sync
        def _(sp):
            sp.dma_start(tokens[:, 0:4, :], x[0].rearrange("(t p) d -> p t d", p=P)).then_inc(x_in, 16)
            sp.dma_start(tokens[:, 4:6, :], ctx[0].rearrange("(t p) d -> p t d", p=P)).then_inc(ctx_in, 16)

            sp.wait_ge(vecs_in, N_VECS * 16)
            for i in range(MOD_FIRST // 4):
                if i >= 3:
                    sp.wait_ge(mod_start_done, i - 2)
                sp.dma_start(mod_start[i % 3][:, :, :],
                             w_mod[0, :, 512 * i:512 * i + 512].rearrange("(k p) n -> p k n", p=P)
                             ).then_inc(mod_start_in[i % 3], 16)

            for l in range(DEPTH):
                for j, (_, _, _, cols) in enumerate(QKV):
                    if j == 4:
                        if l == 0:
                            sp.wait_ge(bias_rows_in, 16)
                        else:
                            sp.wait_ge(bias_ready, 12 * l)
                        for h in range(4):
                            for r in range(ROWS):
                                src = bass.AP(bias_dram.tensor, ((l * 4 + h) * 15 + 7 - r) * 768,
                                              [[48, 16], [768, ROWS], [1, 48]])
                                sp.dma_start(wide[r::ROWS, h, :, :], src).then_inc(wide_in, 16)
                    u = u_in(l) + j
                    if u >= 2:
                        sp.wait_ge(split_ready, u - 1)
                    for half in range(2):
                        sp.dma_start(raw_w[u % 2][:, :, 64 * half:64 * half + 64],
                                     w_in[l, :, cols[half]:cols[half] + 64].rearrange("(k p) n -> p k n", p=P)
                                     ).then_inc(raw_in[u % 2], 16)

                def load_out(u, col):
                    for half in range(2):
                        rows = raw_w[u % 2][64 * half:64 * half + 64]
                        for k0, n, r0, step in ((0, 3, 192 * half, 64), (3, 2, 384 + 64 * half, 128), (5, 3, 640 + 192 * half, 64)):
                            src = bass.AP(w_out.tensor, (l * D + r0) * D + col, [[D, 64], [step * D, n], [1, P]])
                            sp.dma_start(rows[:, k0:k0 + n, :], src).then_inc(raw_in[u % 2], 16)

                for j in range(4):
                    u = u_out(l) + j
                    sp.wait_ge(split_ready, u - 1)
                    load_out(u, P * j)
                if l == 0:
                    sp.wait_ge(unit_done, u_out(0))
                    for n, (ll, m) in enumerate(ATTN_MOD):
                        if n >= 4:
                            sp.wait_ge(mod_done, n - 3)
                        elif n == 2:
                            sp.wait_ge(q_ssq, N_QK)
                        elif n == 3:
                            sp.wait_ge(q_normed, N_QK)
                        sp.dma_start(raw_mod[n % 4][:, :, :],
                                     w_mod[ll, :, P * m:P * m + P].rearrange("(k p) n -> p k n", p=P)
                                     ).then_inc(mod_in[n % 4], 16)
                for j in range(4, KT):
                    u = u_out(l) + j
                    sp.wait_ge(split_ready, u - 1)
                    load_out(u, P * j)
                for ch, n in enumerate(CHUNKS):
                    f0 = sum(CHUNKS[:ch])
                    with sp.Fori(0, n) as f:
                        for side_w, w in enumerate((w_gate, w_up)):
                            sp.wait_ge(split_ready, f * 2 + (u_gate(l, ch) + side_w - 1))
                            sp.dma_start(raw_w[side_w][:, :, :],
                                         w[l].rearrange("(k p) n -> p k n", p=P)[:, :, bass.ds(f * P + f0 * P, P)]
                                         ).then_inc(raw_in[side_w], 16)
                    with sp.Fori(0, KT // 2) as d:
                        for s in range(2):
                            sp.wait_ge(split_ready, d * 2 + (u_down(l, ch) + s - 1))
                            sp.dma_start(raw_w[s][:, 0:n, :],
                                         w_down[l, f0 * P:(f0 + n) * P, :].rearrange("(k p) n -> p k n", p=P)[:, :, bass.ds(d * (2 * P) + s * P, P)]
                                         ).then_inc(raw_in[s], 16)
            for t in range(4):
                sp.wait_ge(y_act if t % 2 == 0 else y_dve, t // 2 + 1)
                sp.dma_start(out[0, P * t:P * t + P, :], tokens[:, t, :]).then_inc(out_in, 16)
            sp.wait_ge(out_in, 64)

        def raw_at(l, stage, i):
            loads = 0
            for ll in range(DEPTH):
                for st, units, each in (("in", 16, 2), ("out", KT, 6)) + tuple(
                        x for ch, n in enumerate(CHUNKS) for x in ((("gate", ch), 2 * n, 1), (("down", ch), KT, 1))):
                    if (ll, st) == (l, stage):
                        return 16 * (loads + each * (i // 2 + 1)) if isinstance(i, int) else 16 * loads
                    loads += each * units // 2

        @block.gpsimd
        def _(pool):
            pool.memset(ones[:, :], 1.0).then_inc(filled, 1)
            pool.memset(eps[:, :], EPS).then_inc(filled, 1)
            pool.memset(zeros[:, :, :], 0.0).then_inc(zeros_set, 1)

            def split(slot, n, landed, used, hi_count):
                pool.wait_ge(raw_in[slot], landed)
                if used is not None:
                    pool.wait_ge(unit_done, used)
                if not isinstance(used, int) and used is not None:
                    pool.tensor_tensor(turnstile[:, 0:1], ones[:, 0:1], ones[:, 0:1], ALU.mult).then_inc(passed, 1)
                pool.tensor_scalar(split_w[slot][:, 0, 0:n, :], raw_w[slot][:, 0:n, :], 1.0, 0.0,
                                   ALU.mult, ALU.add).then_inc(hi_w, 1)
                pool.wait_ge(hi_w, hi_count)
                pool.tensor_tensor(split_w[slot][:, 1, 0:n, :], raw_w[slot][:, 0:n, :],
                                   split_w[slot][:, 0, 0:n, :].bitcast(F32), ALU.subtract).then_inc(split_ready, 1)

            for l in range(DEPTH):
                def rope_cos(j):
                    if not 0 <= j < 16 or QKV[j][0] not in "qk":
                        return
                    i = l * N_ROPE + rope_before(j)
                    pool.wait_ge(q_normed, l * N_QK + qk_before(j) + 1)
                    if i >= 2:
                        pool.wait_ge(q_ready, i - 1)
                    if l == 0 and i == 0:
                        pool.wait_ge(consts_in, N_CONST * 16)
                    pool.tensor_tensor(q_cos[i % 2][:, :], q_n[i % 2][:, :], cos[:, :], ALU.mult).then_inc(q_cos_ready, 1)

                for j in range(16 + 4):
                    u = u_in(l) + j
                    if j < 16:
                        split(u % 2, 8, raw_at(l, "in", j), u - 1 if u >= 2 else None, u + 1)
                    if j < 18:
                        rope_cos(j - 3)
                    if j in (16, 17):
                        split(u % 2, 8, raw_at(l, "out", j - 16), u - 1, u + 1)
                def bias_tables(h):
                    if l == 0 and h == 0:
                        pool.wait_ge(consts_in, N_CONST * 16)
                    if h == 0:
                        pool.wait_ge(wide_in, 16 * 32 * (l + 1))
                        pool.wait_ge(unit_done, u_out(l))
                    pool.tensor_scalar(wide[:, h, :, :], wide[:, h, :, :], 1.0 / SCALE, 0.0,
                                       ALU.mult, ALU.add).then_inc(bias_x8, 1)
                    pool.wait_ge(bias_x8, l * 4 + h + 1)
                    for i in range(3):
                        pool.tensor_tensor(bias[h][:, i, :].rearrange("p (c r) -> p r c", r=ROWS),
                                           wide[:, h, :, BIAS_AT[i]:BIAS_AT[i] + 32],
                                           columns[:, i:i + 1, :].broadcast_to((P, ROWS, 32)), ALU.add
                                           ).then_inc(bias_ready, 1)

                for g in LAYER_STEPS[l]:
                    i, n = g - LAYER_STEPS[l][0], STEPS[g]["n"]
                    pool.wait_ge(exps, g + 1)
                    if i >= 3:
                        pool.wait_ge(prob_ps, g - 2)
                    pool.tensor_scalar(prob16[g % 3][:, 0, 0:n], prob[g % 3][:, 0:n], 1.0, 0.0,
                                       ALU.mult, ALU.add).then_inc(prob_hi, 1)
                    pool.wait_ge(prob_hi, g + 1)
                    pool.tensor_tensor(prob16[g % 3][:, 1, 0:n], prob[g % 3][:, 0:n], prob16[g % 3][:, 0, 0:n],
                                       ALU.subtract).then_inc(prob_lo, 1)
                    if i % 8 == 7 and i // 8 < 4:
                        bias_tables(i // 8)
                for j in range(2, KT):
                    u = u_out(l) + j
                    split(u % 2, 8, raw_at(l, "out", j), u - 1, u + 1)
                for ch, n in enumerate(CHUNKS):
                    with pool.Fori(0, n) as f:
                        for s in range(2):
                            u = u_gate(l, ch) + s
                            split(s, 8, f * 16 + (raw_at(l, ("gate", ch), None) + 16), f * 2 + (u - 1), f * 2 + (u + 1))
                    with pool.Fori(0, KT // 2) as d:
                        for s in range(2):
                            u = u_down(l, ch) + s
                            split(s, n, d * 16 + (raw_at(l, ("down", ch), None) + 16), d * 2 + (u - 1), d * 2 + (u + 1))

        @block.tensor
        def _(pe):
            pe.wait_ge(vecs_in, N_VECS * 16)
            pe.transpose(small[:, 0:P], rows_v[:, :], ident[:, :])
            pe.transpose(small[:, P:P + N_ROWS], rows_c[:, :], ident[0:N_ROWS, 0:N_ROWS]).then_inc(vec_ps, 1)
            pe.wait_ge(x_in, 16)
            pe.wait_ge(ctx_in, 16)
            for k in range(KT):
                if k >= 2:
                    pe.wait_ge(xt_act if k % 2 == 0 else xt_dve, k // 2)
                for t in range(6):
                    mm = pe.transpose(acc[k % 2][:, P * t:P * t + P], tokens[:, t, P * k:P * k + P], ident[:, :])
                mm.then_inc(xt_ps, 1)

            def turn_modulation(n):
                l, m = ATTN_MOD[n]
                pe.wait_ge(mod_row_ready, n + 1)
                pe.transpose(mod_ps[:, 2 * (N_MOD * l + m):2 * (N_MOD * l + m) + 2], mod_row[:, :],
                             ident[0:2, 0:2]).then_inc(mod_turned, 1)

            def modulation(n):
                if n:
                    turn_modulation(n - 1)
                pe.wait_ge(mod_in[n % 4], 16 * (n // 4 + 1))
                for k in range(KT):
                    mm = pe.matmul(mod_ps[0:2, 384:512], silu_c[:, k::KT], raw_mod[n % 4][:, k, :],
                                   start=(k == 0), stop=(k == KT - 1))
                mm.then_inc(mod_done, 1)

            def first_modulations(i):
                pe.wait_ge(mod_start_in[i % 3], 16 * (i // 3 + 1))
                if i >= 2:
                    pe.wait_ge(mod_rows_ready, i - 1)
                ps = (small, mod_ps)[i % 2]
                for k in range(KT):
                    mm = pe.matmul(ps[0:2, :], silu_c[:, k::KT], mod_start[i % 3][:, k, :],
                                   start=(k == 0), stop=(k == KT - 1))
                mm.then_inc(mod_start_done, 1)

            def sum_squares(nu, w):
                if nu == 0:
                    pe.wait_ge(filled, 2)
                pe.wait_ge(ssq_part, (nu + 1) * (KT - 1))
                for a, b in ((0, 512), (512, TOK))[:1 if w == LAT else 2]:
                    mm = pe.matmul(side[:, a:b], ones[:, :], inv[:, a:b], start=True, stop=True)
                mm.then_inc(ssq_done, 1)

            def dense_tile(slot, k, n, moving, w):
                for part in (0, 1, 2):
                    for a, b in ((0, 512), (512, TOK))[:1 if w == LAT else 2]:
                        mm = pe.matmul(acc[slot][:, a:b], split_w[slot][:, part == 2, k, :],
                                       moving[:, part == 1, k, a:b],
                                       start=(k == 0 and part == 0), stop=(k == n - 1 and part == 2))
                if k == n - 1:
                    mm.then_inc(unit_done, 1)

            def dense(slot, n, moving, w, each_k=None):
                for k in range(n):
                    if each_k:
                        each_k(k)
                    dense_tile(slot, k, n, moving, w)

            def dense_pair(w, each_k):
                for k in range(KT + LAG):
                    if k < KT:
                        each_k(k)
                        dense_tile(0, k, KT, act, w)
                    if k >= LAG:
                        dense_tile(1, k - LAG, KT, act, w)

            for l in range(DEPTH):
                if l == 0:
                    pe.wait_ge(silu_c_ready, 1)
                    pe.wait_ge(vec_ready, 1)
                    first_modulations(0)
                sum_squares(2 * l, TOK)
                if l == 0:
                    for i in range(1, MOD_FIRST // 4):
                        first_modulations(i)
                    pe.wait_ge(mod_rows_ready, MOD_FIRST // 4)
                    for m in range(MOD_FIRST):
                        mm = pe.transpose(mod_ps[:, 2 * m:2 * m + 2], mod_rows[:, P * m:P * m + P], ident[0:2, 0:2])
                    mm.then_inc(mod_first, 1)

                def after_copy(j):
                    if not 0 <= j < 16:
                        return
                    kind, t, _, _ = QKV[j]
                    slot = (u_in(l) + j) % 2
                    if j >= 1 and QKV[j - 1][0][0] != "v":
                        pe.wait_ge(q_root, l * N_QK + qk_before(j))
                    elif j >= 1:
                        pe.wait_ge(v_ready, l * 4 + sum(w[0] == "v" for w, *_ in QKV[:j]))
                    if kind[0] == "v":
                        pe.wait_ge(qkv_copied, l * 16 + j + 1)
                        src = raw_q[slot]
                        if kind == "v":
                            for i in range(6):
                                mm = pe.transpose(side[:, P * i:P * i + P], src[:, P * i:P * i + P], ident[:, :])
                        else:
                            if t == 0:
                                pe.wait_ge(q_sin_ready, (l + 1) * N_ROPE)
                            for i in range(8):
                                a = ROWS * SLAB[i // 2] + P * (i % 2)
                                pe.transpose(side[:, P * i:P * i + P], src[:, a:a + P], ident[:, :])
                            for i in range(2):
                                mm = pe.transpose(small[:, P * i:P * i + P], src[:, LAT + P * i:LAT + P * i + P], ident[:, :])
                        mm.then_inc(v_ps, 1)
                    else:
                        pe.wait_ge(q_sq, l * N_QK + qk_before(j) + 1)
                        if kind[0] == "k" or l < DEPTH - 1:
                            pe.matmul(side[:, 512:TOK], pair_ones[:, :], sq[slot][:, 512:TOK], start=True, stop=True)
                        pe.matmul(side[:, 0:512], pair_ones[:, :], sq[slot][:, 0:512], start=True,
                                  stop=True).then_inc(q_ssq, 1)

                def after_norm(j):
                    if not 0 <= j < 16 or QKV[j][0] not in "qk":
                        return
                    i = l * N_ROPE + rope_before(j)
                    pe.wait_ge(q_normed, l * N_QK + qk_before(j) + 1)
                    if i >= 1:
                        pe.wait_ge(q_sin_ready, i)
                    pe.matmul(small[:, 0:LAT], swap[:, :], q_n[i % 2][:, :], start=True, stop=True).then_inc(q_swapped, 1)

                for j in range(16):
                    if j < 16:
                        u = u_in(l) + j
                        pe.wait_ge(split_ready, u + 1)
                        if j >= 2:
                            pe.wait_ge(qkv_copied, l * 16 + j - 1)
                            if QKV[j - 2][0][0] != "v":
                                pe.wait_ge(q_sq, l * N_QK + qk_before(j - 2) + 1)
                        elif l == 0:
                            pe.wait_ge(xt_act, 4)
                            pe.wait_ge(xt_dve, 4)
                        else:
                            pe.wait_ge(resid, 32 * l)
                        if j == 0:
                            pe.wait_ge(split_ready, u + 2)
                            dense_pair(TOK, lambda k: pe.wait_ge(h_lo, 2 * l * KT + k + 1))
                        elif j >= 2:
                            dense(u % 2, 8, act, TOK if QKV[j][0][0] != "q" else width(l))
                    after_norm(j - 2)
                    after_copy(j - 1)

                def score(g):
                    s = STEPS[g]
                    if s["first"]:
                        pe.wait_ge(v_part, 16 * (l + 1))
                        pe.wait_ge(q_ready, N_ROPE * (l + 1))
                        pe.wait_ge(v_ready, 4 * (l + 1))
                        pe.wait_ge(qkv_copied, l * 16 + 15)
                        pe.wait_ge(q_sq, N_QK * (l + 1) - 1)
                        if l == 0:
                            pe.wait_ge(mod_ready, 1)
                    if g - LAYER_STEPS[l][0] == 1:
                        pe.wait_ge(qkv_copied, l * 16 + 16)
                        pe.wait_ge(q_sq, N_QK * (l + 1))
                    if s["group"] == "B":
                        pe.wait_ge(q_normed, N_QK * (l + 1))
                    if g - LAYER_STEPS[l][0] >= 2:
                        pe.wait_ge(exps, g - 1)
                    r = slice(64 * s["half"], 64 * s["half"] + 64)
                    q = qk[r, s["q"], s["q0"]:s["q0"] + P]
                    mm = pe.matmul(acc[g % 2][:, 0:CTX], q, qk[r, s["k"], LAT:TOK], start=True, stop=True)
                    for a in range(0, s["local"], 256):
                        b = min(a + 256, s["local"])
                        mm = pe.matmul(acc[g % 2][:, CTX + a:CTX + b], q, qk[r, s["k"], s["k0"] + a:s["k0"] + b],
                                       start=True, stop=True)
                    mm.then_inc(scores, 1)

                def turn(g):
                    s = STEPS[g]
                    pe.wait_ge(prob_lo, g + 1)
                    if s["first"]:
                        pe.wait_ge(q_root, N_QK * (l + 1))
                    else:
                        pe.wait_ge(prob_t0, g)
                        pe.wait_ge(prob_t1, g)
                    for part in range(2):
                        for t in range(s["n"] // P):
                            mm = pe.transpose(side16[:, 1024 * part + P * t:1024 * part + P * t + P],
                                              prob16[g % 3][:, part, P * t:P * t + P], ident16[:, :])
                    mm.then_inc(prob_ps, 1)

                def weigh(g):
                    s = STEPS[g]
                    pe.wait_ge(prob_t0, g + 1)
                    pe.wait_ge(prob_t1, g + 1)
                    if g > LAYER_STEPS[l][0]:
                        pe.wait_ge(o_summed, g)
                    for t, vc in enumerate(s["v"]):
                        pe.matmul(small[:, 0:192], prob_t[g % 2][:, 0, P * t:P * t + P], v[:, 3 * vc:3 * vc + 192],
                                  start=(t == 0), stop=False)
                        mm = pe.matmul(small[:, 0:128], prob_t[g % 2][:, 1, P * t:P * t + P], v[:, 3 * vc:3 * vc + 128],
                                       start=False, stop=(t == len(s["v"]) - 1))
                    mm.then_inc(o_ps, 1)

                g0, g1 = LAYER_STEPS[l][0], LAYER_STEPS[l][-1] + 1
                for g in range(g0, g1 + 4):
                    if g < g1:
                        score(g)
                        if g == g0:
                            after_copy(15)
                        if g in MOD_AT:
                            modulation(MOD_AT.index(g))
                    if g0 <= g - 3 < g1:
                        turn(g - 3)
                    if g0 <= g - 4 < g1:
                        weigh(g - 4)

                if l == 0:
                    turn_modulation(len(ATTN_MOD) - 1)

                n_t = width(l) // P
                pe.wait_ge(o_ready, g1)

                def outputs_to_features(m):
                    if m >= 2:
                        pe.wait_ge(ot_lo, l * KT + m - 1)
                    for t in range(n_t):
                        mm = pe.transpose((side, acc[1])[m % 2][:, P * t:P * t + P], o[:, t, P * m:P * m + P], ident[:, :])
                    mm.then_inc(ot_ps, 1)

                outputs_to_features(0)

                def output_tile(k):
                    if k + 1 < KT:
                        outputs_to_features(k + 1)
                    pe.wait_ge(ot_lo, l * KT + k + 1)

                for j in range(KT):
                    u = u_out(l) + j
                    pe.wait_ge(split_ready, u + 1)
                    if j == 1:
                        pe.wait_ge(ot_lo, (l + 1) * KT)
                    if j >= 2:
                        pe.wait_ge(resid, 32 * l + j - 1)
                    dense(u % 2, 8, act, width(l), output_tile if j == 0 else None)

                sum_squares(2 * l + 1, width(l))

                for ch, n in enumerate(CHUNKS):
                    f0 = sum(CHUNKS[:ch])
                    pe.wait_ge(resid, 32 * l + KT * (ch + 1) - 1)
                    def late_modulation():
                        for a in range(2):
                            for b in range(2):
                                mm = pe.matmul(small[:, 2 * a + b:2 * a + b + 1], mod_acc[:, b, P * a:P * a + P],
                                               ones[:, 0:1], start=True, stop=True)
                        mm.then_inc(mod_sum, 1)

                    def gate_up(f, before):
                        for s, drained in ((0, silu_done), (1, prod_done)):
                            pe.wait_ge(split_ready, f * 2 + (u_gate(l, ch) + s + 1))
                            if before is not None:
                                pe.wait_ge(drained, before)
                            if s == 1:
                                pe.wait_ge(resid, 32 * l + KT * (ch + 1))
                            dense(s, 8, act, width(l))
                        if l == 0 and before is not None:
                            pe.wait_ge(mod_step, before * 16)
                            late_modulation()

                    def act_tile(k):
                        pe.wait_ge(h_lo, (2 * l + 1) * KT + k + 1)

                    done = l * FT + f0
                    if ch == 0:
                        pe.wait_ge(split_ready, u_gate(l, ch) + 2)
                        if l:
                            pe.wait_ge(silu_done, done)
                            pe.wait_ge(prod_done, done)
                        pe.wait_ge(resid, 32 * l + KT)
                        dense_pair(width(l), act_tile)
                    with pe.Fori(int(ch == 0), n) as f:
                        gate_up(f, f + done)
                    pe.wait_ge(silu_done, l * FT + f0 + n)

                    def hidden_tile(k):
                        if k in (0, n - 1):
                            pe.wait_ge(hid_lo, l * FT + f0 + (n - 1 if k == 0 else n))

                    with pe.Fori(0, KT // 2) as d:
                        for s in range(2):
                            pe.wait_ge(split_ready, d * 2 + (u_down(l, ch) + s + 1))
                            pe.wait_ge(resid, d * 2 + (32 * l + KT * (ch + 1) + s - 1))
                            dense(s, n, hidden, width(l), hidden_tile)
                if l == 0:
                    pe.wait_ge(mod_step, 16 * FT)
                    late_modulation()

            for t in range(4):
                pe.wait_ge(resid, 32 * DEPTH)
                if t >= 2:
                    pe.wait_ge(y_act if t % 2 == 0 else y_dve, t // 2)
                for k in range(KT):
                    mm = pe.transpose(acc[t % 2][:, P * k:P * k + P], x_t[:, k, P * t:P * t + P], ident[:, :])
                mm.then_inc(y_ps, 1)

        @block.scalar
        def _(sc):
            sc.dma_start(ident[:, :], k_ident[:, :]).then_inc(vecs_in, 16)
            sc.dma_start(rows_c[0:KT, :], c[0].rearrange("(k p) -> k p", p=P)).then_inc(vecs_in, 16)
            sc.dma_start(rows_c[KT:2 * KT, :], c_ctx.rearrange("(k p) -> k p", p=P)).then_inc(vecs_in, 16)
            for half in range(2):
                sc.dma_start(rows_c[2 * KT:N_ROWS, 64 * half:64 * half + 64], qk_norm.rearrange("l g d -> (l g) d")
                             ).then_inc(vecs_in, 16)
            for l in range(DEPTH):
                r = 64 * l
                sc.dma_start(rows_v[r:r + 48, :], b_mod[l].rearrange("(k p) -> k p", p=P)).then_inc(vecs_in, 16)
                sc.dma_start(rows_v[r + 48:r + 56, :], norm_attn[l].rearrange("(k p) -> k p", p=P)).then_inc(vecs_in, 16)
                sc.dma_start(rows_v[r + 56:r + 64, :], norm_ffn[l].rearrange("(k p) -> k p", p=P)).then_inc(vecs_in, 16)
            for dst, src in ((pair_ones, k_pairs), (swap, k_swap), (cos, k_cos), (sin, k_sin)):
                sc.dma_start(dst[:, :], src[:, :]).then_inc(consts_in, 16)
            sc.dma_start(window[:, :, :], k_window[:, :, :]).then_inc(consts_in, 16)
            sc.dma_start(columns[:, :, :], k_columns[:, :, :]).then_inc(consts_in, 16)
            sc.dma_start(sinks[:, :], bass.AP(sink.tensor, 0, [[0, P], [1, DEPTH * 6]])).then_inc(consts_in, 16)
            sc.wait_ge(zeros_set, 1)
            n_rows = DEPTH * 4 * 15
            sc.dma_start(bias_dram.rearrange("a (b c) -> a b c", c=64), zeros[0:n_rows, :, :].broadcast_to((n_rows, 12, 64))).then_inc(zero_in, 16)
            sc.wait_ge(zero_in, 16)
            sc.dma_start(bass.AP(bias_dram.tensor, 1, [[768, n_rows], [49, 16], [1, 31]]),
                         bass.AP(rpb.tensor, 0, [[31, n_rows], [0, 16], [1, 31]])).then_inc(bias_rows_in, 16)

            sc.wait_ge(vec_ready, 1)
            sc.activation(silu_c[:, :], vecs[:, P:P + 2 * KT], ACT.Silu).then_inc(silu_c_ready, 1)
            for k in range(0, KT, 2):
                sc.wait_ge(xt_ps, k + 1)
                sc.activation(x_t[:, k, :], acc[0][:, 0:TOK], ACT.Copy).then_inc(xt_act, 1)

            def squares(nu, w, ready):
                for k in range(KT):
                    ready(k)
                    if k == 0:
                        if nu % 2:
                            sc.wait_ge(q_normed, N_QK * (nu // 2 + 1))
                        elif nu:
                            sc.wait_ge(scaled_ready, nu * KT)
                    elif k >= 3:
                        sc.wait_ge(ssq_part, nu * (KT - 1) + k - 2)
                    elif nu % 2:
                        sc.wait_ge(q_ssq, N_QK * (nu // 2 + 1))
                    elif nu:
                        sc.wait_ge(ssq_part, nu * (KT - 1))
                    dst = sq[k % 2] if k else inv
                    sc.activation(dst[:, 0:w], x_t[:, k, 0:w], ACT.Square).then_inc(sq_ready, 1)

            def take_norm_root(nu, w):
                sc.wait_ge(ssq_done, nu + 1)
                if nu:
                    sc.wait_ge(q_inv, N_QK * ((nu + 1) // 2))
                    sc.wait_ge(inv_ready, nu)
                sc.activation(root[:, 0:w], side[:, 0:w], ACT.Sqrt, bias=eps[:, 0:1], scale=1.0 / D).then_inc(root_ready, 1)

            def shifted(nu, l, w):
                for k in range(KT):
                    sc.wait_ge(scaled_ready, nu * KT + k + 1)
                    for b, a0_, a1_ in parts(w):
                        i = sc.activation(act[:, 0, k, a0_:a1_], scaled[k % 2][:, a0_:a1_], ACT.Identity,
                                          bias=mod[:, l, 3 * KT * (nu % 2) + k, b:b + 1])
                    i.then_inc(h_hi, 1)

            for l in range(DEPTH):
                def ready(k, l=l):
                    if l == 0:
                        sc.wait_ge(xt_act if k % 2 == 0 else xt_dve, k // 2 + 1)
                        if k == 0:
                            sc.wait_ge(filled, 2)
                    else:
                        sc.wait_ge(resid, 32 * l - KT + k + 1)
                squares(2 * l, TOK, ready)
                take_norm_root(2 * l, TOK)
                if l == 0:
                    for i in range(MOD_FIRST // 4):
                        sc.wait_ge(mod_start_done, i + 1)
                        sc.activation(mod_rows[:, 512 * i:512 * i + 512], (small, mod_ps)[i % 2][0:2, :],
                                      ACT.Copy).then_inc(mod_rows_ready, 1)
                shifted(2 * l, l, TOK)

                def take_root(j):
                    if not 0 <= j < 16 or QKV[j][0][0] == "v":
                        return
                    i = l * N_QK + qk_before(j)
                    w = TOK if QKV[j][0][0] == "k" else width(l)
                    sc.wait_ge(q_ssq, i + 1)
                    if qk_before(j):
                        sc.wait_ge(q_inv, i)
                    else:
                        sc.wait_ge(inv_ready, 2 * l + 1)
                    sc.activation(root[:, 0:w], side[:, 0:w], ACT.Sqrt, bias=eps[:, 0:1], scale=1.0 / HD).then_inc(q_root, 1)

                for j in range(17):
                    if j < 16:
                        kind, t, _, _ = QKV[j]
                        slot = (u_in(l) + j) % 2
                        w = TOK if kind[0] != "q" else width(l)
                        sc.wait_ge(unit_done, u_in(l) + j + 1)
                        if j >= 2 and QKV[j - 2][0][0] == "v":
                            sc.wait_ge(v_ps, l * 4 + sum(w_[0] == "v" for w_, *_ in QKV[:j - 1]))
                        elif j >= 2:
                            sc.wait_ge(q_normed, l * N_QK + qk_before(j - 1))
                        if kind == "vb":
                            sc.activation(by_col(raw_q[slot][:, 0:LAT]), acc[slot][:, 0:LAT].rearrange("p (r c) -> p r c", r=ROWS), ACT.Copy)
                            sc.activation(raw_q[slot][:, LAT:TOK], acc[slot][:, LAT:TOK], ACT.Copy).then_inc(qkv_copied, 1)
                        else:
                            sc.activation(raw_q[slot][:, 0:w], acc[slot][:, 0:w], ACT.Copy).then_inc(qkv_copied, 1)
                        if kind[0] != "v":
                            if qk_before(j) >= 2:
                                sc.wait_ge(q_ssq, l * N_QK + qk_before(j) - 1)
                            else:
                                sc.wait_ge(ssq_part, (2 * l + 1) * (KT - 1))
                            sc.activation(sq[slot][:, 0:w], acc[slot][:, 0:w], ACT.Square).then_inc(q_sq, 1)
                    take_root(j - 1)

                def softmax(g):
                    s = STEPS[g]
                    i, n, li = g - LAYER_STEPS[l][0], s["n"], s["layer"] * 6 + s["head"]
                    sc.wait_ge(neg_top, g + 1)
                    if i >= 3:
                        sc.wait_ge(prob_lo, g - 2)
                    sc.activation(prob[g % 3][:, 0:n], acc[g % 2][:, 0:n], ACT.Exp, bias=stat[:, 1, i:i + 1],
                                  scale=SCALE, accum_out=stat[:, 2, i:i + 1]).then_inc(exps, 1)
                    if s["sink"]:
                        sc.activation(stat[:, 3, i:i + 1], sinks[:, li:li + 1], ACT.Exp,
                                      bias=stat[:, 1, i:i + 1]).then_inc(sink_exp, 1)

                def copy_turned(g):
                    n = STEPS[g]["n"]
                    sc.wait_ge(prob_ps, g + 1)
                    if g - LAYER_STEPS[l][0] >= 2:
                        sc.wait_ge(o_ps, g - 1)
                    sc.activation(prob_t[g % 2][:, 0, 0:n], side16[:, 0:n], ACT.Copy).then_inc(prob_t0, 1)

                g0, g1 = LAYER_STEPS[l][0], LAYER_STEPS[l][-1] + 1
                for g in range(g0, g1 + 3):
                    if g0 <= g - 3:
                        copy_turned(g - 3)
                    if g < g1:
                        softmax(g)
                    if g in MOD_AT:
                        sc.wait_ge(mod_done, MOD_AT.index(g) + 1)
                        sc.activation(mod_row[:, :], mod_ps[0:2, 384:512], ACT.Copy).then_inc(mod_row_ready, 1)

                w = width(l)
                for m in range(KT):
                    sc.wait_ge(ot_ps, l * KT + m + 1)
                    if m in (3, 4):
                        i = sc.activation(act[:, 0, m, 0:LAT].rearrange("p (r c) -> p c r", r=ROWS),
                                          (side, acc[1])[m % 2][:, 0:LAT].rearrange("p (c r) -> p c r", r=ROWS), ACT.Copy)
                        if w == TOK:
                            i = sc.activation(act[:, 0, m, LAT:TOK], (side, acc[1])[m % 2][:, LAT:TOK], ACT.Copy)
                    else:
                        i = sc.activation(act[:, 0, m, 0:w], (side, acc[1])[m % 2][:, 0:w], ACT.Copy)
                    i.then_inc(ot_hi, 1)

                squares(2 * l + 1, w, lambda k: sc.wait_ge(resid, 32 * l + k + 1))
                take_norm_root(2 * l + 1, w)
                shifted(2 * l + 1, l, w)

                for ch, n in enumerate(CHUNKS):
                    f0 = sum(CHUNKS[:ch])
                    def gated(f, before):
                        sc.wait_ge(unit_done, f * 2 + (u_gate(l, ch) + 1))
                        sc.activation(silu_g[0][:, 0:w], acc[0][:, 0:w], ACT.Silu).then_inc(silu_done, 1)
                        if l == 0:
                            if before is not None:
                                sc.wait_ge(mod_step, before * 16)
                            sc.dma_start(mod_chunk[:, :, :],
                                         w_mod[1].rearrange("(k p) n -> p k n", p=P)[:, :, bass.ds(f * (2 * P) + f0 * 2 * P, 2 * P)]
                                         ).then_inc(mod_chunk_in, 16)
                        sc.wait_ge(prod_done, f + (l * FT + f0 + 1))
                        sc.activation(hidden[:, 0, bass.ds(f, 1), 0:w].rearrange("p a t -> p (a t)"), prod[0][:, 0:w], ACT.Copy).then_inc(hid_hi, 1)

                    done = l * FT + f0
                    if done == 0:
                        gated(0, None)
                    with sc.Fori(int(done == 0), n) as f:
                        gated(f, f + f0)

            for t in range(0, 4, 2):
                sc.wait_ge(y_ps, t + 1)
                sc.activation(tokens[:, t, :], acc[0][:, :], ACT.Copy).then_inc(y_act, 1)

        @block.vector
        def _(ve):
            ve.wait_ge(vec_ps, 1)
            ve.tensor_copy(vecs[:, :], small[:, 0:P + N_ROWS]).then_inc(vec_ready, 1)
            ve.wait_ge(consts_in, N_CONST * 16)
            ve.tensor_scalar(neg_sinks[:, :], sinks[:, :], -1.0, SHIFT, ALU.mult, ALU.add).then_inc(neg_ready, 1)
            ve.tensor_copy(ident16[:, :], ident[:, :]).then_inc(ident16_ready, 1)
            for k in range(1, KT, 2):
                ve.wait_ge(xt_ps, k + 1)
                ve.tensor_copy(x_t[:, k, :], acc[1][:, 0:TOK]).then_inc(xt_dve, 1)

            def modulations(n, l, m0, m1):
                b = vecs[:, 64 * l + m0:64 * l + m1].rearrange("p (m a) -> p m a", a=1).broadcast_to((P, m1 - m0, 2))
                ps = mod_ps[:, 2 * (N_MOD * l + m0):2 * (N_MOD * l + m1)].rearrange("p (m a) -> p m a", a=2)
                ve.tensor_tensor(mod[:, l, m0:m1, :], ps, b, ALU.add).then_inc(mod_ready, 1)

            def gains(l, which):
                m0 = KT * (1 + 3 * which)
                g = vecs[:, 64 * l + 48 + KT * which:64 * l + 56 + KT * which].rearrange("p (m a) -> p m a", a=1).broadcast_to((P, KT, 2))
                ve.scalar_tensor_tensor(out=gain[:, l, which, :, :], in0=mod[:, l, m0:m0 + KT, :], scalar=1.0, in1=g,
                                        op0=ALU.add, op1=ALU.mult).then_inc(gain_ready, 1)

            ve.wait_ge(vec_ready, 1)
            def add_square(nu, k, w):
                ve.wait_ge(sq_ready, nu * KT + k + 1)
                if k >= 2:
                    ve.wait_ge(ssq_part, nu * (KT - 1) + k - 1)
                ve.tensor_tensor(inv[:, 0:w], inv[:, 0:w], sq[k % 2][:, 0:w], ALU.add).then_inc(ssq_part, 1)

            for k in range(1, KT):
                add_square(0, k, TOK)

            def normed(nu, l, w):
                ve.wait_ge(root_ready, nu + 1)
                ve.reciprocal(inv[:, 0:w], root[:, 0:w]).then_inc(inv_ready, 1)
                ve.wait_ge(inv_ready, nu + 1)
                if nu == 0:
                    ve.wait_ge(mod_first, 1)
                    modulations(0, 0, 0, MOD_FIRST)
                    ve.wait_ge(mod_ready, 1)
                    gains(0, 0)
                ve.wait_ge(gain_ready, [1, 2, 4, 4][nu])
                if nu == 0:
                    ve.wait_ge(xt_act, 4)

                def lo(k):
                    ve.wait_ge(h_hi, nu * KT + k + 1)
                    for b, a0_, a1_ in parts(w):
                        i = ve.scalar_tensor_tensor(out=act[:, 1, k, a0_:a1_], in0=scaled[k % 2][:, a0_:a1_],
                                                    scalar=mod[:, l, 3 * KT * (nu % 2) + k, b:b + 1],
                                                    in1=act[:, 0, k, a0_:a1_].bitcast(F32), op0=ALU.add, op1=ALU.subtract)
                    i.then_inc(h_lo, 1)

                for k in range(KT):
                    if k >= 2:
                        ve.wait_ge(h_lo, nu * KT + k - 1)
                    for b, a0_, a1_ in parts(w):
                        i = ve.scalar_tensor_tensor(out=scaled[k % 2][:, a0_:a1_], in0=x_t[:, k, a0_:a1_],
                                                    scalar=gain[:, l, nu % 2, k, b:b + 1], in1=inv[:, a0_:a1_],
                                                    op0=ALU.mult, op1=ALU.mult)
                    i.then_inc(scaled_ready, 1)
                    if k:
                        lo(k - 1)
                lo(KT - 1)

            def residual(slot, xk, l, gate_tile, w):
                for b, a0_, a1_ in parts(w):
                    i = ve.scalar_tensor_tensor(out=xk[:, a0_:a1_], in0=acc[slot][:, a0_:a1_], scalar=gate_tile[:, b:b + 1],
                                                in1=xk[:, a0_:a1_], op0=ALU.mult, op1=ALU.add)
                i.then_inc(resid, 1)

            for l in range(DEPTH):
                w = width(l)
                normed(2 * l, l, TOK)

                def norm_tile(j, deferred=None):
                    if not 0 <= j < 16:
                        return
                    kind, t, grp, _ = QKV[j]
                    slot = (u_in(l) + j) % 2
                    if kind[0] == "v":
                        i = sum(w_[0] == "v" for w_, *_ in QKV[:j])
                        ve.wait_ge(v_ps, l * 4 + i + 1)
                        nb = 12 if kind == "v" else 20
                        b0_ = V_AT[t if kind == "v" else 2 + t] // HD
                        pieces = [(0, 12, side, 0)] if kind == "v" else [(0, 16, side, 0), (16, 20, small, 0)]
                        out_ = v[:, 192 * b0_:192 * (b0_ + nb)].rearrange("p (b s d) -> p b s d", s=3, d=HD)
                        rest = v_rest[:, 0:nb * HD].rearrange("p (b d) -> p b d", d=HD)
                        done = 4 * (l * 4 + i)
                        for b_, e_, ps, at_ in pieces:
                            mm = ve.tensor_copy(out_[:, b_:e_, 0, :], ps[:, 0:(e_ - b_) * HD].rearrange("p (b d) -> p b d", d=HD))
                        mm.then_inc(v_part, 1)
                        ve.wait_ge(v_part, done + 1)
                        ve.wait_ge(h_lo, (2 * l + 1) * KT)
                        for b_, e_, ps, at_ in pieces:
                            mm = ve.tensor_tensor(rest[:, b_:e_, :], ps[:, 0:(e_ - b_) * HD].rearrange("p (b d) -> p b d", d=HD),
                                                  out_[:, b_:e_, 0, :], ALU.subtract)
                        mm.then_inc(v_ready, 1)
                        ve.wait_ge(v_ready, l * 4 + i + 1)
                        ve.tensor_copy(out_[:, :, 1, :], rest).then_inc(v_part, 1)
                        ve.wait_ge(v_part, done + 2)
                        ve.tensor_tensor(out_[:, :, 2, :], rest, out_[:, :, 1, :], ALU.subtract).then_inc(v_part, 2)
                        return
                    i = l * N_QK + qk_before(j)
                    wq = TOK if kind[0] == "k" else w
                    ve.wait_ge(q_root, i + 1)
                    if qk_before(j):
                        ve.wait_ge(q_normed, i)
                    if deferred == 0:
                        ve.reciprocal(inv[:, 0:wq // 2], root[:, 0:wq // 2])
                        return
                    a = 0 if deferred is None else wq // 2
                    ve.reciprocal(inv[:, a:wq], root[:, a:wq]).then_inc(q_inv, 1)
                    ve.wait_ge(q_inv, i + 1)
                    g = vecs[:, P + 2 * KT + l * 6 + grp:P + 2 * KT + l * 6 + grp + 1]
                    raw = raw_q[slot]
                    ve.wait_ge(qkv_copied, l * 16 + j + 1)
                    if wq == TOK:
                        ve.scalar_tensor_tensor(out=qk[:, t, LAT:TOK], in0=raw[:, LAT:TOK], scalar=g, in1=inv[:, LAT:TOK],
                                                op0=ALU.mult, op1=ALU.mult)
                    if kind in "qk":
                        r = l * N_ROPE + rope_before(j)
                        if r >= 2:
                            ve.wait_ge(q_ready, r - 1)
                        ve.scalar_tensor_tensor(out=q_n[r % 2][:, :], in0=raw[:, 0:LAT], scalar=g, in1=inv[:, 0:LAT],
                                                op0=ALU.mult, op1=ALU.mult).then_inc(q_normed, 1)
                    else:
                        rc = dict(r=ROWS)
                        ve.scalar_tensor_tensor(out=qk[:, t, 0:LAT].rearrange("p (c r) -> p c r", **rc),
                                                in0=raw[:, 0:LAT].rearrange("p (r c) -> p c r", **rc), scalar=g,
                                                in1=inv[:, 0:LAT].rearrange("p (r c) -> p c r", **rc),
                                                op0=ALU.mult, op1=ALU.mult).then_inc(q_normed, 1)

                def rotate(j):
                    if not 0 <= j < 16 or QKV[j][0] not in "qk":
                        return
                    kind, t, _, _ = QKV[j]
                    r = l * N_ROPE + rope_before(j)
                    ve.wait_ge(q_swapped, r + 1)
                    if r:
                        ve.wait_ge(q_ready, r)
                    ve.tensor_tensor(q_sin[:, :], small[:, 0:LAT], sin[:, :], ALU.mult).then_inc(q_sin_ready, 1)
                    ve.wait_ge(q_sin_ready, r + 1)
                    ve.wait_ge(q_cos_ready, r + 1)
                    ve.tensor_tensor(qk[:, t, 0:LAT], q_cos[r % 2][:, :], q_sin[:, :], ALU.add).then_inc(q_ready, 1)

                for j in range(1, 16):
                    rotate(j - 2)
                    norm_tile(j - 1)

                def top_of(g):
                    s = STEPS[g]
                    i, n, li = g - LAYER_STEPS[l][0], s["n"], s["layer"] * 6 + s["head"]
                    ve.wait_ge(scores, g + 1)
                    for col, which in s["masks"]:
                        part = acc[g % 2][:, col:col + P]
                        ve.tensor_tensor(part, part, window[:, which, :], ALU.add).then_inc(fixed, 1)
                    if s["bias"]:
                        var = VARIANT[s["qb"]]
                        ve.wait_ge(bias_ready, 12 * l + 3 * s["head"] + 3)
                        part = acc[g % 2][:, CTX:CTX + 256]
                        ve.tensor_tensor(part, part, bias[s["head"]][:, var, :], ALU.add).then_inc(fixed, 1)
                    if n_fix(s):
                        ve.wait_ge(fixed, upto(g + 1, n_fix))
                    ve.reduce_max(stat[:, 0, i:i + 1], acc[g % 2][:, 0:n], AX_X).then_inc(top, 1)

                def minus_top(g):
                    s, i = STEPS[g], g - LAYER_STEPS[l][0]
                    ve.wait_ge(top, g + 1)
                    ve.tensor_scalar(stat[:, 1, i:i + 1], stat[:, 0, i:i + 1], -SCALE, SHIFT, ALU.mult,
                                     ALU.add).then_inc(neg_raw if s["sink"] else neg_top, 1)

                def with_sink(g):
                    s, i = STEPS[g], g - LAYER_STEPS[l][0]
                    li = s["layer"] * 6 + s["head"]
                    if s["sink"]:
                        ve.wait_ge(neg_raw, upto(g + 1, is_sink))
                        ve.tensor_scalar(stat[:, 1, i:i + 1], stat[:, 1, i:i + 1], neg_sinks[:, li:li + 1], None,
                                         ALU.min).then_inc(neg_top, 1)

                def copy_turned(g):
                    n = STEPS[g]["n"]
                    ve.wait_ge(prob_ps, g + 1)
                    if g - LAYER_STEPS[l][0] >= 2:
                        ve.wait_ge(o_ps, g - 1)
                    ve.tensor_copy(prob_t[g % 2][:, 1, 0:n], side16[:, 1024:1024 + n]).then_inc(prob_t1, 1)

                def add_sink(g):
                    s = STEPS[g]
                    i = g - LAYER_STEPS[l][0]
                    ve.wait_ge(exps, g + 1)
                    if s["sink"]:
                        ve.wait_ge(sink_exp, upto(g + 1, is_sink))
                        ve.tensor_tensor(stat[:, 3, i:i + 1], stat[:, 2, i:i + 1], stat[:, 3, i:i + 1], ALU.add).then_inc(denom, 1)

                def denominator(g):
                    s = STEPS[g]
                    i = g - LAYER_STEPS[l][0]
                    if s["sink"]:
                        ve.wait_ge(denom, upto(g + 1, is_sink))
                    src = stat[:, 3 if s["sink"] else 2, i:i + 1]
                    ve.reciprocal(stat[:, 4, i:i + 1], src).then_inc(r_denom, 1)

                def sum_output(g):
                    ve.wait_ge(o_ps, g + 1)
                    if g > LAYER_STEPS[0][0]:
                        ve.wait_ge(o_ready, g)
                    ve.tensor_reduce(o_sum[:, :], small[:, 0:3 * HD].rearrange("p (s d) -> p d s", s=3), AX_X,
                                     ALU.add).then_inc(o_summed, 1)

                def take_output(g):
                    s = STEPS[g]
                    i = g - LAYER_STEPS[l][0]
                    ve.wait_ge(r_denom, g + 1)
                    ve.wait_ge(o_summed, g + 1)
                    ve.tensor_scalar(o[:, s["qt"], s["o"]:s["o"] + HD], o_sum[:, :], stat[:, 4, i:i + 1], None,
                                     ALU.mult).then_inc(o_ready, 1)

                g0, g1 = LAYER_STEPS[l][0], LAYER_STEPS[l][-1] + 1
                for g in range(g0, g1 + 5):
                    new, turned, last = g < g1, g0 <= g - 3 < g1, g0 <= g - 5
                    if new:
                        top_of(g)
                    if new:
                        minus_top(g)
                    if last:
                        take_output(g - 5)
                    if new:
                        with_sink(g)
                    if turned:
                        add_sink(g - 3)
                    if g - g0 in (2, 3):
                        norm_tile(15, g - g0 - 2)
                    if turned:
                        copy_turned(g - 3)
                        denominator(g - 3)
                    if g0 <= g - 4 < g1:
                        sum_output(g - 4)

                if l == 0:
                    ve.wait_ge(mod_turned, len(ATTN_MOD))
                    modulations(1, 0, MOD_FIRST, N_MOD)
                    modulations(2, 1, N_FFN_MOD, N_MOD)
                    ve.wait_ge(mod_ready, 3)
                    gains(0, 1)

                for m in range(KT):
                    ve.wait_ge(ot_hi, l * KT + m + 1)
                    if m in (3, 4):
                        i = ve.tensor_tensor(act[:, 1, m, 0:LAT].rearrange("p (r c) -> p c r", r=ROWS),
                                             (side, acc[1])[m % 2][:, 0:LAT].rearrange("p (c r) -> p c r", r=ROWS),
                                             act[:, 0, m, 0:LAT].rearrange("p (r c) -> p c r", r=ROWS).bitcast(F32), ALU.subtract)
                        if w == TOK:
                            i = ve.tensor_tensor(act[:, 1, m, LAT:TOK], (side, acc[1])[m % 2][:, LAT:TOK],
                                                 act[:, 0, m, LAT:TOK].bitcast(F32), ALU.subtract)
                    else:
                        i = ve.tensor_tensor(act[:, 1, m, 0:w], (side, acc[1])[m % 2][:, 0:w], act[:, 0, m, 0:w].bitcast(F32), ALU.subtract)
                    i.then_inc(ot_lo, 1)

                for j in range(KT):
                    ve.wait_ge(unit_done, u_out(l) + j + 1)
                    residual(j % 2, x_t[:, j, :], l, mod[:, l, 2 * KT + j, :], w)
                    if j >= 2:
                        add_square(2 * l + 1, j - 1, w)
                add_square(2 * l + 1, KT - 1, w)

                normed(2 * l + 1, l, w)

                for ch, n in enumerate(CHUNKS):
                    f0 = sum(CHUNKS[:ch])
                    def product(f, before):
                        if before is not None:
                            ve.wait_ge(hid_lo, before)
                        ve.wait_ge(unit_done, f * 2 + (u_gate(l, ch) + 2))
                        ve.wait_ge(silu_done, f + (l * FT + f0 + 1))
                        ve.tensor_tensor(prod[0][:, 0:w], acc[1][:, 0:w], silu_g[0][:, 0:w], ALU.mult).then_inc(prod_done, 1)
                        ve.wait_ge(hid_hi, f + (l * FT + f0 + 1))
                        ve.tensor_tensor(hidden[:, 1, bass.ds(f, 1), 0:w].rearrange("p a t -> p (a t)"), prod[0][:, 0:w],
                                         hidden[:, 0, bass.ds(f, 1), 0:w].rearrange("p a t -> p (a t)").bitcast(F32),
                                         ALU.subtract).then_inc(hid_lo, 1)

                    def add_late(f, before):
                        ve.wait_ge(mod_sum, before)
                        m = f * 2 + (2 * f0 - 2)
                        ve.tensor_tensor(mod[:, 1, bass.ds(m, 2), :], small[:, 0:4].rearrange("p (a b) -> p a b", b=2),
                                         vecs[:, bass.ds(m + 64, 2)].rearrange("p (m a) -> p m a", a=1).broadcast_to((P, 2, 2)),
                                         ALU.add).then_inc(mod_late, 1)

                    def late_modulation(f, before):
                        ve.wait_ge(mod_chunk_in, f * 16 + 16 * (f0 + 1))
                        for k in range(KT):
                            for b in range(2):
                                if before is not None or k:
                                    ve.wait_ge(mod_step, f * 16 + (16 * f0 + 2 * k + b - 1 + (k == 0) * (1 - b)))
                                kw = dict(out=mod_acc[:, b, :], in0=mod_chunk[:, k, :], scalar=silu_c[:, b * KT + k:b * KT + k + 1])
                                if k == 0:
                                    i = ve.tensor_scalar(kw["out"], kw["in0"], kw["scalar"], None, ALU.mult)
                                else:
                                    i = ve.scalar_tensor_tensor(**kw, in1=mod_acc[:, b, :], op0=ALU.mult, op1=ALU.add)
                                i.then_inc(mod_step, 1)

                    done = l * FT + f0
                    if done == 0:
                        product(0, None)
                        late_modulation(0, None)
                    with ve.Fori(int(done == 0), n) as f:
                        product(f, f + done)
                        if l == 0:
                            add_late(f, f + f0)
                            late_modulation(f, f + f0)
                    if ch == len(CHUNKS) - 1 and l < DEPTH - 1:
                        for j in range(KT):
                            ve.wait_ge(unit_done, u_down(l, ch) + j + 1)
                            residual(j % 2, x_t[:, j, :], l, mod[:, l, 5 * KT + j, :], w)
                            if j >= 2:
                                add_square(2 * l + 2, j - 1, w)
                        add_square(2 * l + 2, KT - 1, w)
                        continue
                    with ve.Fori(0, KT // 2) as d:
                        for s in range(2):
                            ve.wait_ge(unit_done, d * 2 + (u_down(l, ch) + s + 1))
                            residual(s, x_t[:, bass.ds(d * 2 + s, 1), :].rearrange("p a t -> p (a t)"), l,
                                     mod[:, l, bass.ds(d * 2 + (5 * KT + s), 1), :].rearrange("p a t -> p (a t)"), w)

                if l == 0:
                    ve.wait_ge(mod_sum, FT)
                    m = N_FFN_MOD - 2
                    ve.tensor_tensor(mod[:, 1, m:m + 2, :], small[:, 0:4].rearrange("p (a b) -> p a b", b=2),
                                     vecs[:, 64 + m:66 + m].rearrange("p (m a) -> p m a", a=1).broadcast_to((P, 2, 2)),
                                     ALU.add).then_inc(mod_late, 1)
                    ve.wait_ge(mod_late, FT)
                    ve.wait_ge(mod_step, 16 * FT)
                    gains(1, 0)
                    gains(1, 1)

            for t in range(1, 4, 2):
                ve.wait_ge(y_ps, t + 1)
                ve.tensor_copy(tokens[:, t, :], acc[1][:, :]).then_inc(y_dve, 1)


N_ROWS = 2 * KT + DEPTH * 6
N_VECS = 5 + 3 * DEPTH
N_CONST = 7


def shape_constants():
    f = np.float32
    p = np.arange(P)
    ident = np.eye(P, dtype=f)
    pairs = (p[:, None] // 64 == p[None, :] // 64).astype(f)
    swap = (p[:, None] == (p[None, :] ^ 32)).astype(f)
    t = np.arange(LAT)
    inv = (f(10000.0) ** (-np.arange(16, dtype=f) / f(16))).astype(f)
    ang = np.concatenate([(t // GRID_W).astype(f)[:, None] * inv, (t % GRID_W).astype(f)[:, None] * inv], 1)
    cos = np.ascontiguousarray(np.cos(ang).astype(f).T[p % 32])
    sin = np.ascontiguousarray(np.sin(ang).astype(f).T[p % 32] * np.where(p % 64 < 32, f(-1), f(1))[:, None])
    i = np.arange(P)
    window = np.stack([np.where(i[None, :] >= i[:, None], 0, NEG), np.where(i[None, :] <= i[:, None], 0, NEG)], 1).astype(f)
    columns = np.zeros((P, 3, 32), f)
    for cb in (0, 1, 3):
        col = 16 * cb + p // ROWS
        first = np.clip(col - 8, 0, GRID_W - 16)
        key = SLAB[cb] + np.arange(32)
        ok = (key[None, :] >= first[:, None]) & (key[None, :] < first[:, None] + 16)
        columns[:, VARIANT[cb]] = np.where(ok, 0, NEG)
    return {"k_ident": ident, "k_pairs": pairs, "k_swap": swap, "k_cos": cos, "k_sin": sin.astype(f),
            "k_window": window, "k_columns": columns}


_INS = ['x', 'c', 'ctx', 'c_ctx', 'w_mod', 'b_mod', 'norm_attn', 'norm_ffn', 'w_in', 'qk_norm', 'sink', 'rpb',
        'w_out', 'w_gate', 'w_up', 'w_down']


def kernel(**inputs):
    import concourse.bacc as _bacc
    from concourse.bass_utils import run_bass_kernel_spmd as _run

    nc = _bacc.Bacc("TRN2", target_bir_lowering=False, num_devices=1)
    consts = shape_constants()
    arrays, args = {}, []
    for name in _INS + list(consts):
        a = np.ascontiguousarray(inputs[name] if name in inputs else consts[name])
        arrays[f"in_{name}"] = a
        args.append(nc.dram_tensor(f"in_{name}", a.shape, mybir.dt.from_np(a.dtype), kind="ExternalInput").ap())
    args.append(nc.dram_tensor("out_0", (1, LAT, D), F32, kind="ExternalOutput").ap())
    trunk(nc, *args)
    r = _run(nc, [arrays], core_ids=[0])
    return r.results[0]["out_0"]
```
